# Optimizing a Trainium2 kernel written in Bass

```python
import math
import jax, jax.numpy as jnp
from jax import lax
import numpy as np

D_MODEL = 1024
BATCH = 1
SEQ = 1024
DEPTH = 2
DEC_BATCH = 8
DEC_SEQ = 4
PAST_LEN = 4096
PAGE_SIZE = 128

N_MIXERS = 2
HEAD_DIM = 64
A_HEADS = 12
A_KV_HEADS = 4
A_GROUP = A_HEADS // A_KV_HEADS
WINDOW = 128
BLOCK = 128
W_BUF = min(WINDOW, PAST_LEN)
B_WIDTH = 768
B_GROUPS = 4
B_GROUP_DIM = B_WIDTH // B_GROUPS
CHUNK = 128
X_HEADS = 4
X_WIDTH = X_HEADS * HEAD_DIM
N_MEM = 256
D_FF = 2816
CONV_W = 3
N_A = (DEPTH + 1) // 2
N_B = DEPTH // 2
A_Q = A_HEADS * HEAD_DIM
A_KV = A_KV_HEADS * HEAD_DIM
A_IN = A_Q + 2 * A_KV + X_WIDTH
A_OUT = A_Q + X_WIDTH
B_IN = 2 * B_WIDTH + X_WIDTH
B_OUT = B_WIDTH + X_WIDTH
EPS = 1e-6
NEG = -1e30

kernel_name = 'swa_sink_gmlp_chunk_memattn_convffn_step'

def rms_norm(x, g):
    xf = x.astype(jnp.float32)
    y = xf * lax.rsqrt(jnp.mean(xf * xf, axis=-1, keepdims=True) + EPS)
    return (y * g.astype(jnp.float32)).astype(x.dtype)

def alibi_slopes(n):
    def pow2(m):
        start = 2.0 ** (-8.0 / m)
        return [start ** (i + 1) for i in range(m)]
    p = 2 ** int(math.floor(math.log2(n)))
    s = pow2(p)
    if p < n:
        s = s + pow2(2 * p)[0::2][: n - p]
    return jnp.asarray(s, jnp.float32)

def sink_gqa_attention(q, k, v, dist, valid, slopes, sinks):
    *lead, nq, _, hd = q.shape
    qg = q.reshape(*lead, nq, A_KV_HEADS, A_GROUP, hd)
    s = jnp.einsum('...qhgd,...khd->...hgqk', qg, k).astype(jnp.float32) * (hd ** -0.5)
    s = s - slopes.reshape(A_KV_HEADS, A_GROUP, 1, 1) * dist[..., None, None, :, :]
    s = jnp.where(valid[..., None, None, :, :], s, NEG)
    sink = sinks.astype(jnp.float32).reshape(A_KV_HEADS, A_GROUP, 1, 1)
    m = jnp.maximum(jnp.max(s, axis=-1, keepdims=True), sink)
    e = jnp.exp(s - m)
    p = e / (jnp.sum(e, axis=-1, keepdims=True) + jnp.exp(sink - m))
    o = jnp.einsum('...hgqk,...khd->...qhgd', p.astype(v.dtype), v)
    return o.reshape(*lead, nq, A_HEADS * hd)

def swa_prompt(q, k, v, slopes, sinks):
    n, t = q.shape[:2]
    nb = t // BLOCK
    qb = q.reshape(n, nb, BLOCK, A_HEADS, HEAD_DIM)

    def band(x):
        xb = x.reshape(n, nb, BLOCK, A_KV_HEADS, HEAD_DIM)
        prev = jnp.pad(xb[:, :-1], ((0, 0), (1, 0), (0, 0), (0, 0), (0, 0)))
        return jnp.concatenate([prev, xb], axis=2)

    i = jnp.arange(BLOCK)[:, None]
    j = jnp.arange(2 * BLOCK)[None, :]
    d = i + BLOCK - j
    kpos = jnp.arange(nb)[:, None, None] * BLOCK - BLOCK + j[None]
    valid = (d >= 0) & (d < WINDOW) & (kpos >= 0)
    dist = jnp.broadcast_to(d.astype(jnp.float32), valid.shape)
    o = sink_gqa_attention(qb, band(k), band(v), dist[None], valid[None], slopes, sinks)
    return o.reshape(n, t, A_Q)

def swa_sample(q, k_new, v_new, k_buf, v_buf, slopes, sinks):
    s = q.shape[1]
    k = jnp.concatenate([k_buf, k_new], axis=1)
    v = jnp.concatenate([v_buf, v_new], axis=1)
    i = jnp.arange(s)[:, None]
    j = jnp.arange(W_BUF + s)[None, :]
    d = i + W_BUF - j
    valid = (d >= 0) & (d < WINDOW)
    o = sink_gqa_attention(q, k, v, d.astype(jnp.float32)[None], valid[None], slopes, sinks)
    return o, k[:, -W_BUF:], v[:, -W_BUF:]

def chunk_spatial_gate(u, vn, w_s, b_s):
    n, t, _ = vn.shape
    L = min(t, CHUNK)
    vc = vn.reshape(n, t // L, L, B_GROUPS, B_GROUP_DIM)
    w = jnp.tril(w_s[:, :L, :L])
    mixed = jnp.einsum('gij,ncjgd->ncigd', w, vc) + b_s[:, :L].T[None, None, :, :, None]
    return u * mixed.reshape(n, t, B_WIDTH)

def memory_kv(mem, g, w, kg):
    n, m, _ = mem.shape
    kv = rms_norm(mem, g) @ w
    mk, mv = jnp.split(kv, 2, axis=-1)
    mk = rms_norm(mk.reshape(n, m, X_HEADS, HEAD_DIM), kg)
    return mk, mv.reshape(n, m, X_HEADS, HEAD_DIM)

def memory_attention(q, mk, mv):
    n, t = q.shape[:2]
    s = jnp.einsum('nthd,nmhd->nhtm', q, mk).astype(jnp.float32) * (HEAD_DIM ** -0.5)
    p = jax.nn.softmax(s, axis=-1)
    o = jnp.einsum('nhtm,nmhd->nthd', p.astype(mv.dtype), mv)
    return o.reshape(n, t, X_WIDTH)

def conv_ffn(x, g, w_in, conv_w, conv_b, w_down, prefix):
    t = x.shape[1]
    gu = rms_norm(x, g) @ w_in
    a, up = jnp.split(gu, 2, axis=-1)
    full = jnp.concatenate([prefix, a], axis=1)
    c = conv_b + sum(conv_w[r] * full[:, r:r + t] for r in range(CONV_W))
    y = (jax.nn.silu(c) * up) @ w_down
    return y, full[:, -(CONV_W - 1):]

def run_group(x, p, is_prompt, mem=None, mem_k_in=None, mem_v_in=None,
              win_k_in=None, win_v_in=None, conv_in=None):
    n, t, _ = x.shape
    slopes = alibi_slopes(A_HEADS)
    win_k, win_v, chunk_v, mem_ks, mem_vs, convs = [], [], [], [], [], []
    for i in range(DEPTH):
        if is_prompt:
            mk, mv = memory_kv(mem, p['mem_norm_g'][i], p['w_mem_kv'][i], p['xk_norm'][i])
            mem_ks.append(mk)
            mem_vs.append(mv)
        else:
            mk, mv = mem_k_in[i], mem_v_in[i]
        h = rms_norm(x, p['norm1_g'][i])
        if i % N_MIXERS == 0:
            a = i // N_MIXERS
            z = h @ p['w_in_a'][a]
            q, k, v, xq = jnp.split(z, [A_Q, A_Q + A_KV, A_Q + 2 * A_KV], axis=-1)
            q = rms_norm(q.reshape(n, t, A_HEADS, HEAD_DIM), p['q_norm_a'][a])
            k = rms_norm(k.reshape(n, t, A_KV_HEADS, HEAD_DIM), p['k_norm_a'][a])
            v = v.reshape(n, t, A_KV_HEADS, HEAD_DIM)
            if is_prompt:
                o = swa_prompt(q, k, v, slopes, p['sinks_a'][a])
                nk, nv = k[:, t - W_BUF:], v[:, t - W_BUF:]
            else:
                o, nk, nv = swa_sample(q, k, v, win_k_in[a], win_v_in[a], slopes, p['sinks_a'][a])
            win_k.append(nk)
            win_v.append(nv)
            w_out = p['w_out_a'][a]
        else:
            b = i // N_MIXERS
            z = h @ p['w_in_b'][b]
            uv, xq = z[..., :2 * B_WIDTH], z[..., 2 * B_WIDTH:]
            u, v = jnp.split(jax.nn.gelu(uv, approximate=False), 2, axis=-1)
            vn = rms_norm(v, p['v_norm_b'][b])
            o = chunk_spatial_gate(u, vn, p['w_s_b'][b], p['b_s_b'][b])
            chunk_v.append(vn[:, ((t - 1) // CHUNK) * CHUNK:])
            w_out = p['w_out_b'][b]
        xq = rms_norm(xq.reshape(n, t, X_HEADS, HEAD_DIM), p['xq_norm'][i])
        xo = memory_attention(xq, mk, mv)
        x = x + jnp.concatenate([o, xo], axis=-1) @ w_out
        prefix = jnp.zeros((n, CONV_W - 1, D_FF), x.dtype) if is_prompt else conv_in[i]
        yf, cst = conv_ffn(x, p['norm2_g'][i], p['w_ffn_in'][i], p['conv_w'][i],
                           p['conv_b'][i], p['w_down'][i], prefix)
        convs.append(cst)
        x = x + yf
    return (x, jnp.stack(win_k), jnp.stack(win_v), jnp.stack(chunk_v),
            mem_ks, mem_vs, jnp.stack(convs))

def setup_inputs(seed: int = 0) -> dict:
    key = jax.random.key(seed)
    ks = jax.random.split(key, 32)
    f32 = jnp.float32
    res = (2 * DEPTH) ** -0.5

    def nrm(k, shape, scale):
        return jax.random.normal(k, shape, f32) * scale

    def gain(k, shape):
        return 1.0 + 0.02 * jax.random.normal(k, shape, f32)

    return {
        'x_prompt': nrm(ks[0], (BATCH, SEQ, D_MODEL), 1.0),
        'x_sample': nrm(ks[1], (DEC_BATCH, DEC_SEQ, D_MODEL), 1.0),
        'cache_win_k': nrm(ks[2], (N_A, DEC_BATCH, W_BUF, A_KV_HEADS, HEAD_DIM), 1.0),
        'cache_win_v': nrm(ks[3], (N_A, DEC_BATCH, W_BUF, A_KV_HEADS, HEAD_DIM), 1.0),
        'cache_mem_k': nrm(ks[4], (DEPTH, DEC_BATCH, N_MEM, X_HEADS, HEAD_DIM), 1.0),
        'cache_mem_v': nrm(ks[5], (DEPTH, DEC_BATCH, N_MEM, X_HEADS, HEAD_DIM), 1.0),
        'state_conv': nrm(ks[6], (DEPTH, DEC_BATCH, CONV_W - 1, D_FF), 1.0),
        'mem_prompt': nrm(ks[7], (BATCH, N_MEM, D_MODEL), 1.0),
        'norm1_g': gain(ks[8], (DEPTH, D_MODEL)),
        'norm2_g': gain(ks[9], (DEPTH, D_MODEL)),
        'mem_norm_g': gain(ks[10], (DEPTH, D_MODEL)),
        'w_in_a': nrm(ks[11], (N_A, D_MODEL, A_IN), D_MODEL ** -0.5),
        'q_norm_a': gain(ks[12], (N_A, HEAD_DIM)),
        'k_norm_a': gain(ks[13], (N_A, HEAD_DIM)),
        'sinks_a': nrm(ks[14], (N_A, A_HEADS), 0.5),
        'w_out_a': nrm(ks[15], (N_A, A_OUT, D_MODEL), A_OUT ** -0.5 * res),
        'w_in_b': nrm(ks[16], (N_B, D_MODEL, B_IN), D_MODEL ** -0.5),
        'v_norm_b': gain(ks[17], (N_B, B_WIDTH)),
        'w_s_b': nrm(ks[18], (N_B, B_GROUPS, CHUNK, CHUNK), CHUNK ** -0.5),
        'b_s_b': gain(ks[19], (N_B, B_GROUPS, CHUNK)),
        'w_out_b': nrm(ks[20], (N_B, B_OUT, D_MODEL), B_OUT ** -0.5 * res),
        'w_mem_kv': nrm(ks[21], (DEPTH, D_MODEL, 2 * X_WIDTH), D_MODEL ** -0.5),
        'xq_norm': gain(ks[22], (DEPTH, HEAD_DIM)),
        'xk_norm': gain(ks[23], (DEPTH, HEAD_DIM)),
        'w_ffn_in': nrm(ks[24], (DEPTH, D_MODEL, 2 * D_FF), D_MODEL ** -0.5),
        'conv_w': nrm(ks[25], (DEPTH, CONV_W, D_FF), CONV_W ** -0.5),
        'conv_b': nrm(ks[26], (DEPTH, D_FF), 0.02),
        'w_down': nrm(ks[27], (DEPTH, D_FF, D_MODEL), D_FF ** -0.5 * res),
    }

def reference(x_prompt, x_sample, cache_win_k, cache_win_v, cache_mem_k, cache_mem_v,
              state_conv, mem_prompt, norm1_g, norm2_g, mem_norm_g, w_in_a, q_norm_a,
              k_norm_a, sinks_a, w_out_a, w_in_b, v_norm_b, w_s_b, b_s_b, w_out_b,
              w_mem_kv, xq_norm, xk_norm, w_ffn_in, conv_w, conv_b, w_down):
    p = dict(norm1_g=norm1_g, norm2_g=norm2_g, mem_norm_g=mem_norm_g, w_in_a=w_in_a,
             q_norm_a=q_norm_a, k_norm_a=k_norm_a, sinks_a=sinks_a, w_out_a=w_out_a,
             w_in_b=w_in_b, v_norm_b=v_norm_b, w_s_b=w_s_b, b_s_b=b_s_b, w_out_b=w_out_b,
             w_mem_kv=w_mem_kv, xq_norm=xq_norm, xk_norm=xk_norm, w_ffn_in=w_ffn_in,
             conv_w=conv_w, conv_b=conv_b, w_down=w_down)
    (y_prompt, win_k_prompt, win_v_prompt, chunk_v_prompt, mem_ks, mem_vs,
     conv_prompt) = run_group(x_prompt, p, True, mem=mem_prompt)
    mem_k_prompt = jnp.stack(mem_ks)
    mem_v_prompt = jnp.stack(mem_vs)
    (y_sample, win_k_sample, win_v_sample, chunk_v_sample, _, _,
     conv_sample) = run_group(x_sample, p, False, mem_k_in=cache_mem_k, mem_v_in=cache_mem_v,
                              win_k_in=cache_win_k, win_v_in=cache_win_v, conv_in=state_conv)
    return (y_prompt, y_sample, win_k_prompt, win_v_prompt, chunk_v_prompt, mem_k_prompt,
            mem_v_prompt, conv_prompt, win_k_sample, win_v_sample, chunk_v_sample, conv_sample)


_drawn_inputs = setup_inputs


def setup_inputs(seed=0):
    import zlib

    import numpy as np

    out = dict(_drawn_inputs(seed))
    spreads = {}
    factors = {'norm1_g': 2.717,
     'mem_norm_g': 2.832,
     'q_norm_a': 8.0,
     'k_norm_a': 2.791,
     'sinks_a': 18.777,
     'v_norm_b': 8.466,
     'b_s_b': 25.116,
     'xq_norm': 23.095,
     'conv_b': 7.178,
     'norm2_g': 2.689}
    for name, (base, spread) in spreads.items():
        noise = np.random.default_rng([zlib.crc32(name.encode()), seed]).standard_normal(out[name].shape)
        drawn = base * np.exp(spread * noise) if base else spread * noise
        out[name] = __import__('jax').numpy.asarray(drawn.astype(out[name].dtype))
    for name, factor in factors.items():
        out[name] = (out[name] * factor).astype(out[name].dtype)
    return out
```

```python
from contextlib import ExitStack

import concourse.bass as bass
from concourse import mybir

F32 = mybir.dt.float32
F32R = mybir.dt.float32r
ACT = mybir.ActivationFunctionType
ALU = mybir.AluOpType
AX = mybir.AxisListType.X

P = 128
D_MODEL = 1024
KD = D_MODEL // P
SEQ = 1024
DEC_BATCH = 8
DEC_SEQ = 4
TS = DEC_BATCH * DEC_SEQ
T = TS + SEQ
NCH = 3
CH = T // NCH
BLOCK = 128
NB = SEQ // BLOCK
HD = 64
A_KV = 4
N_MEM = 256
D_FF = 2816
NF = D_FF // P
NG = NF // 2
EPS = 1e-6

N_MEMU = 8
IN_A, IN_B, OUT_U = 12, 14, 8
FFN_UNITS = 3 * NF
R_INA = N_MEMU
R_OUTA = R_INA + IN_A
R_FFN = [R_OUTA + OUT_U, 0]
R_INB = R_FFN[0] + 2 * NF
R_OUTB = R_INB + IN_B
R_FFN[1] = R_OUTB + OUT_U
S_INA = N_MEMU
S_OUTA = S_INA + IN_A
S_FFN = [S_OUTA + OUT_U, 0]
S_INB = S_FFN[0] + FFN_UNITS
S_OUTB = S_INB + IN_B
S_FFN[1] = S_OUTB + OUT_U
N_STREAM = S_FFN[1] + FFN_UNITS

SEL_ALL = 10
ALL_ROW = 20
NSEL = 11
N_SSQ = (KD - 1) * NCH
X_PIECES = [0, 0, 3, 6, 9, 12, 16, 20, 24]
LAG = 3
RING = LAG + 1
KEYS_S = BLOCK + TS


def unit_tiles(layer):
    return list(range(IN_A)) if layer == 0 else [12, 13, *range(6, 12), *range(6)]


def stat_tiles(layer):
    return list(range(10)) if layer == 0 else unit_tiles(1)[0:8]


def sel_of(layer, t):
    return t if layer == 0 else SEL_ALL if t < 12 else t - 12


def sample_items(layer):
    return ([("swa", j) for j in range(3)] if layer == 0 else []) + [("mem", 0)]


def spreads_a():
    return [(q // NCH, q % NCH, 1 + q % 5, q - 4 if q >= 5 else None) for q in range(30)]


def spread_b(q):
    parts = [6 * (i + 1) if i < NCH else 18 + i - NCH + 1 for i in range(9)]
    s_i, for_tiles = (SEL_ALL, list(range(6, 12))) if q < NCH else (q // NCH - 1, [11 + q // NCH])
    return s_i, q % NCH, 6 + q % 2, parts[q - 2] if q >= 2 else None, for_tiles


def piece(w, e):
    return (e % NCH, e // NCH) if w == 0 else (e // KD, e % KD)


def piece_index(w, c, k):
    return NCH * k + c if w == 0 else KD * c + k


def swa_items(layer):
    out = []
    for b in range(NB):
        if layer == 0:
            out += [("swa", b, g) for g in range(A_KV)]
        out += [("mem", b, p) for p in range(2)]
    return out


def hybrid_step(nc, d, o, slopes):
    ctx = ExitStack()
    with ctx:
        cursor = [(nc.sbuf_base + 31) // 32 * 32]

        def size(shape):
            n = 4
            for s in shape[1:]:
                n *= s
            return (n + 31) // 32 * 32

        def put(name, shape, dt=F32):
            t = nc.alloc_sbuf_tensor_at(name, shape, dt, offset=cursor[0])
            cursor[0] += size(shape)
            return t

        def sem(name):
            return ctx.enter_context(nc.semaphore(name))

        x = put("x", [P, KD, T])
        raw = put("raw", [P, 2, D_MODEL])
        w_hi = put("w_hi", [P, 2, D_MODEL], F32R)
        w_lo = put("w_lo", [P, 2, D_MODEL], F32R)
        ident = put("ident", [P, P])
        sel = put("sel", [P, NSEL, 32])
        gain = put("gain", [P, 6, KD])
        hgain = put("hgain", [P, 6])
        qgain = put("qgain", [P, 3])
        vgain = put("vgain", [P, 6])
        cols = put("cols", [P, 8])
        sink_p = put("sink_p", [P, 12])
        sink_s = put("sink_s", [P, 3])
        nsink_p = put("nsink_p", [P, 12])
        nsink_s = put("nsink_s", [P, 3])
        conv_c = put("conv_c", [P, 2, NF, 4])
        state_in = put("state_in", [P, NF, 16])
        state_out = put("state_out", [P, NF, 18])
        mem_k = put("mem_k", [P, 4, N_MEM])
        mem_v = put("mem_v", [P, 2, 2, 256])
        h_at = cursor[0]
        h_hi = put("h_hi", [P, KD, T], F32R)
        h_lo = put("h_lo", [P, KD, T], F32R)
        r_at = cursor[0]
        cursor[0] = h_at
        s_k = put("s_k", [P, 2, DEC_BATCH, KEYS_S])
        s_v = put("s_v", [P, DEC_BATCH, 256])
        s_mk = [put("s_mk", [P, 2, DEC_BATCH, N_MEM])] * 2
        s_mv = [put("s_mv", [P, 2, DEC_BATCH, 256])] * 2
        q_pad = put("q_pad", [P, 17 * P])
        s_p = put("s_p", [P, 4, N_MEM])
        sp_t = put("sp_t", [P, 5, P])
        assert cursor[0] <= r_at
        cursor[0] = r_at
        mem_x = put("mem_x", [P, KD, N_MEM])
        hm_hi = [put(f"hm_hi{l}", [P, KD, N_MEM], F32R) for l in range(2)]
        hm_lo = [put(f"hm_lo{l}", [P, KD, N_MEM], F32R) for l in range(2)]
        Z_OVER_MEM = (cursor[0] - r_at) // size([P, T])
        mem_ssq = put("mem_ssq", [P, N_MEM])
        mem_root_t = put("mem_root_t", [32, N_MEM])
        mem_rstd = put("mem_rstd", [32, N_MEM])
        mem_rb = put("mem_rb", [P, N_MEM])
        mk_raw = put("mk_raw", [P, 4, N_MEM])
        mk_sq = put("mk_sq", [P, 4, N_MEM])
        mv_t = put("mv_t", [P, 4, N_MEM])
        mem_end = cursor[0]
        cursor[0] = r_at
        z = put("z", [P, IN_B, T])
        assert cursor[0] <= r_at + 50688 + 9216
        cursor[0] = r_at + size([P, IN_A, T])
        v_tok = put("v_tok", [P, NB + 1, 256])
        assert mem_end <= cursor[0]
        sel_t = put("sel_t", [3 * 32, NSEL, P])
        keep_at = cursor[0]
        nd_p = put("nd_p", [P, 2 * BLOCK])
        nd_s = put("nd_s", [P, KEYS_S])
        mix_at = cursor[0]
        z_sq = put("z_sq", [P, 2, T])
        cursor[0] = mix_at
        mem_sq = put("mem_sq", [P, KD, N_MEM])
        cursor[0] = mix_at
        s_exp = put("s_exp", [P, RING, 3 * 256])
        stat = put("stat", [P, 4, 6, 3])
        o_s = put("o_s", [P, KD, TS])
        k_tok = put("k_tok", [TS, 256])
        sp_new = put("sp_new", [TS, 3, P])
        s_stat = put("s_stat", [P, 6, 4])
        end_a = cursor[0]
        cursor[0] = r_at + 10 * size([P, T])
        p_t = put("p_t", [P, 2, 2 * 3 * P])
        cursor[0] = keep_at
        ws_t = put("ws_t", [P, 4, P])
        ws4 = put("ws4", [TS, 4, TS])
        bb = put("bb", [P, 6, P])
        bb4 = put("bb4", [P, 6, TS])
        gate_at = cursor[0]
        z_sq1 = put("z_sq1", [P, 2, T])
        cursor[0] = gate_at
        vn_tok = put("vn_tok", [P, 2, 768])
        mixed = put("mixed", [P, 2, 6 * P])
        cursor[0] = gate_at
        s_exp1 = put("s_exp1", [P, RING, 2 * 256])
        p_t1 = put("p_t1", [P, 2, 2 * 2 * P])
        end_b = max(cursor[0], gate_at + 4 * 3072)
        cursor[0] = end_b
        stat1 = put("stat1", [P, 4, 6, 3])
        o_s1 = put("o_s1", [P, KD, TS])
        s_stat1 = put("s_stat1", [P, 6, 4])
        end_b = cursor[0]
        cursor[0] = r_at
        d_hi = put("d_hi", [P, 2, D_MODEL], F32R)
        d_lo = put("d_lo", [P, 2, D_MODEL], F32R)
        g_hi = put("g_hi", [P, 2, T], F32R)
        g_lo = put("g_lo", [P, 2, T], F32R)
        a_buf = put("a_buf", [P, 2, 48 + 2 + SEQ])
        c_buf = put("c_buf", [P, 2, T])
        g_f = put("g_f", [P, T])
        assert cursor[0] <= keep_at - size([P, NSEL, P])
        top = nc.sbuf_usable_end // 32 * 32
        cursor[0] = top - (2 * size([P, T]) + size([P, 4, CH]) + 2 * size([P, CH]))
        assert cursor[0] >= mix_at, (cursor[0], mix_at)
        ssq = put("ssq", [P, T])
        sq_ring = put("sq_ring", [P, 4, CH])
        root = put("root", [96, CH])
        rstd = put("rstd", [96, CH])
        rb_at = cursor[0]
        rb = put("rb", [P, T])
        assert mix_at + size([P, 2, T]) <= rb_at and gate_at + size([P, 2, T]) <= rb_at
        assert end_a <= top and end_b <= top, (end_a, end_b, top)

        ps = ctx.enter_context(nc.psum_tensor("ps", [P, 8, 512], F32))

        def banks(b, n, width):
            return ps[:, b:b + n, :].rearrange("p b n -> p (b n)")[:, 0:width]

        consts = sem("consts_landed")
        consts2 = sem("sel_t_landed")
        x_landed = [sem(f"x_landed{j}") for j in range(4)]
        mem_landed = sem("mem_landed")
        state_landed = sem("state_landed")
        raw_landed = [sem(f"raw_landed{s}") for s in range(2)]
        hi_cut = sem("hi_cut")
        prepped = sem("units_prepared")
        proj = sem("chunks_projected")
        freed = [sem(f"chunks_taken{s}") for s in range(2)]
        squared = sem("squares_written")
        ssq_added = sem("squares_added")
        ssq_sum = sem("square_sums")
        rooted = sem("roots_written")
        recip = sem("rstd_written")
        spread = sem("rstd_spread")
        rb_taken = sem("rstd_of_tokens_written")
        h_cut = sem("h_high_parts")
        h_ready = sem("h_low_parts")
        outs = sem("outputs_written")
        state_stored = sem("conv_state_written")
        neg = sem("constants_derived")

        n_out = [0]
        mem_sqd, mem_sum, mem_st, mem_root, mem_rs, mem_bc = (sem(f"mem_{n}") for n in
            ("squared", "summed", "stat", "root", "rstd", "spread"))
        mem_hc, mem_hr = (sem(f"mem_h_{n}") for n in ("high", "ready"))
        mem_rbt, mem_stored = sem("mem_rstd_of_tokens_written"), sem("mem_v_stored")
        mem_kn, mem_vt = sem("mem_k_normed"), sem("mem_v_turned")
        mem_vd = sem("mem_v_taken")
        mem_ksq = sem("mem_k_squared")

        mx = []
        gate_names = ("gate_in", "masked", "gate_turned", "gate_taken", "gate_mixed", "gate_biased", "gate_mult",
                      "gate_cut", "gate_done", "gelud")
        for l in range(2):
            names = ("z_sq", "z_stat", "z_root", "z_rstd", "z_spread", "z_normed", "turned", "turned_taken",
                     "caches", "qpad_zeroed", "qpad_filled", "s_scores", "s_biased", "s_max", "s_exped", "s_recip",
                     "s_normed", "s_turned", "s_turned_taken", "s_pv", "s_pv_taken", "s_cut", "s_done",
                     "s_keys", "scored", "biased", "maxed", "maxed2", "ready", "exped", "summed", "recip",
                     "normed", "pturned", "pturned_taken", "pv", "o_cut", "o_done", "gate_in", "masked",
                     "gate_turned", "gate_taken", "gate_mixed", "gate_biased", "gate_mult", "gate_cut", "gate_done",
                     "gelud")
            mx.append({n: sem(f"{n}{l}") for n in names if l == 1 or n not in gate_names})

        a_pre, c0_done, conv1, conv_done, silued, c_scaled, g_cut, g_done = (
            [sem(f"{n}{l}") for l in range(2)] for n in
            ("prefix_copied", "conv_started", "conv_tap1", "conv_done", "silu_done", "silu_scaled", "g_high",
             "g_ready"))
        dn_done, dn_added = sem("down_projected"), sem("down_added")
        zeroed = sem("conv_padding_zeroed")
        st_copied = sem("conv_state_copied")

        CONST_LOADS = [("ident", ident), ("sel", sel), ("gain", gain), ("hgain", hgain), ("vgain", vgain),
                       ("cols", cols), ("sink_p", sink_p), ("sink_s", sink_s), ("conv_c", conv_c),
                       ("nd_p", nd_p), ("nd_s", nd_s)]
        NCONST = len(CONST_LOADS)

        def o_view(item, n, buf):
            kind, b, g = item
            t0 = TS + b * BLOCK
            if kind == "mem":
                return buf[:, 6 + g, t0:t0 + BLOCK], ps[:, 6 + n % 2, 0:P]
            i, half = g // 2, g % 2
            rows = slice(64 * half, 64 * half + 64)
            return (buf[rows, 3 * i:3 * i + 3, t0:t0 + BLOCK],
                    ps[rows, 6 + n % 2, 0:3 * P].rearrange("p (j n) -> p j n", j=3))

        sp_tm = sp_t[:, 3:5, :]

        block = ctx.enter_context(nc.Block())

        @block.sync
        def _(sp):
            for s in range(2):
                sp.dma_start(raw[:, s], d["w"][s]).then_inc(raw_landed[s], 16)
            with sp.Fori(1, N_STREAM // 2) as i:
                for s in range(2):
                    sp.wait_ge(prepped, 2 * i + s - 1)
                    sp.dma_start(raw[:, s:s + 1], d["w"][bass.ds(2 * i + s, 1)].rearrange("o p n -> p o n")) \
                      .then_inc(raw_landed[s], 16)

        @block.gpsimd
        def _(pool):
            def low(slot, n, hi, lo):
                pool.wait_ge(hi_cut, n + 1)
                pool.tensor_tensor(lo, raw[:, slot], hi.bitcast(F32), ALU.subtract).then_inc(prepped, 1)

            def low_up(n, slot_n, slot_r):
                low(slot_n, n, w_hi[:, slot_r], w_lo[:, slot_r])

            def low_down(n, slot_n, q):
                low(slot_n, n, d_hi[:, q], d_lo[:, q])

            def add_squares(w, parts):
                for p in parts:
                    c = p % NCH
                    pool.wait_ge(squared, (N_SSQ + NCH) * w + NCH + p + 1)
                    if p >= NCH:
                        pool.wait_ge(ssq_added, N_SSQ * w + p - 2)
                    ch = ssq[:, c * CH:(c + 1) * CH]
                    pool.tensor_tensor(ch, ch, sq_ring[:, p % 4], ALU.add).then_inc(ssq_added, 1)

            def low_pairs(n0, pairs):
                with pool.Fori(0, pairs) as i:
                    for s in range(2):
                        low_up(2 * i + n0 + s, s, s)

            def low_out_and_add(w, s_out, s_ffn):
                for oo in range(KD):
                    n = s_out + oo + 2 if oo + 2 < OUT_U else s_ffn + oo + 2 - OUT_U
                    if oo < KD - 1:
                        low_up(n, n % 2, oo % 2)
                    if oo >= 1:
                        add_squares(w, range(NCH * (oo - 1), NCH * oo))
                    if oo == KD - 1:
                        low_up(n, n % 2, oo % 2)

            def low_ffn(l):
                n0 = S_FFN[l]
                low_up(n0 + 2, n0 % 2, 0)
                with pool.Fori(0, NG - 1) as i:
                    n = 6 * i + n0
                    low_up(n + 3, (n0 + 3) % 2, 1)
                    low_up(n + 4, (n0 + 4) % 2, 0)
                    low_down(n + 5, (n0 + 5) % 2, 0)
                    low_down(n + 6, (n0 + 6) % 2, 1)
                    low_up(n + 7, (n0 + 7) % 2, 1)
                    low_up(n + 8, (n0 + 8) % 2, 0)
                n = n0 + 6 * (NG - 1)
                low_up(n + 3, (n + 3) % 2, 1)
                low_down(n + 4, (n + 4) % 2, 0)
                low_down(n + 5, (n + 5) % 2, 1)

            low_pairs(0, (S_OUTA + 2) // 2)
            for l in range(2):
                m = mx[l]
                pool.wait_ge(proj, 3 * ((R_INA + IN_A) if l == 0 else (R_INB + IN_B)))
                pool.memset(q_pad[:, :], 0.0).then_inc(m["qpad_zeroed"], 1)
                se, st = (s_exp, stat) if l == 0 else (s_exp1, stat1)
                for n, (kind, b, g) in enumerate(swa_items(l)):
                    w = BLOCK if kind == "swa" and b == 0 else 256
                    nh = 3 if kind == "swa" else 2
                    pool.wait_ge(m["recip"], n + 1)
                    for hh in range(nh):
                        v = se[:, n % RING, hh * 256:hh * 256 + w]
                        ins = pool.tensor_scalar(v, v, st[:, n % 4, 5, hh:hh + 1], 1.0, ALU.mult, ALU.mult)
                    ins.then_inc(m["normed"], 1)
                if l == 0:
                    low_out_and_add(1, S_OUTA, S_FFN[0])
                    low_ffn(0)
                    low_pairs(S_INB, 1)
                    add_squares(2, range(N_SSQ))
                    low_pairs(S_INB + 2, IN_B // 2 - 1)
                    mg = mx[1]
                    pool.wait_ge(mg["gate_in"], 16 * 4)
                    pool.affine_select(out=ws_t[:, :, :], in_=ws_t[:, :, :], compare_op=ALU.is_ge, fill=0.0, base=0,
                                       pattern=[[0, 4], [1, P]], channel_multiplier=-1).then_inc(mg["masked"], 1)
                    pool.affine_select(out=ws4[:, :, :], in_=ws4[:, :, :], compare_op=ALU.is_ge, fill=0.0, base=0,
                                       pattern=[[0, 4], [1, TS]], channel_multiplier=-1).then_inc(mg["masked"], 1)
                    low_pairs(S_OUTB, 1)
                else:
                    low_out_and_add(3, S_OUTB, S_FFN[1])
                    low_ffn(1)

        @block.tensor
        def _(pe):
            def products(out, hi_w, lo_w, hi_x, lo_x, ks, first=True, last=True, landed=None):
                ins = None
                for n, k in enumerate(ks):
                    if landed is not None:
                        landed(k)
                    a, b = hi_w(k), lo_w(k)
                    pe.matmul(out, a, hi_x(k), start=(first and n == 0), stop=False)
                    pe.matmul(out, a, lo_x(k), start=False, stop=False)
                    ins = pe.matmul(out, b, hi_x(k), start=False, stop=(last and n == len(ks) - 1))
                return ins

            def unit(n, r, slot, w=None, early=None, after=None):
                pe.wait_ge(prepped, n + 1)
                for c in range(NCH):
                    pe.wait_ge(freed[slot], 3 * r + c - 2)
                    if early is not None:
                        early(c)
                    t0 = c * CH
                    landed = None if w is None else \
                        (lambda k: pe.wait_ge(h_ready, KD * NCH * w + piece_index(w, c, k) + 1))
                    products(ps[:, 3 * slot + c, 0:CH],
                             lambda k: w_hi[:, slot, k * P:(k + 1) * P], lambda k: w_lo[:, slot, k * P:(k + 1) * P],
                             lambda k: h_hi[:, k, t0:t0 + CH], lambda k: h_lo[:, k, t0:t0 + CH],
                             range(KD), landed=landed).then_inc(proj, 1)
                    if after is not None:
                        after(c)

            def norm_stat(w):
                pe.wait_ge(ssq_added, N_SSQ * (w + 1))
                for c in range(NCH):
                    mm = pe.matmul(ps[32 * c:32 * c + 32, 7, 0:CH], sel[:, SEL_ALL, :], ssq[:, c * CH:(c + 1) * CH],
                                   start=True, stop=True)
                mm.then_inc(ssq_sum, 1)

            def norm_spread(w, c):
                pe.wait_ge(recip, w + 1)
                if c == 2:
                    pe.wait_ge(rb_taken, NCH * w + 1)
                pe.matmul(ps[:, 6 + c % 2, 0:CH], sel_t[32 * c:32 * c + 32, SEL_ALL, :], rstd[32 * c:32 * c + 32, :],
                          start=True, stop=True).then_inc(spread, 1)

            def first_units(w, n, r, early=None):
                unit(n, r, 0, w=w)
                norm_stat(w)

                def after(c):
                    if c == 1:
                        norm_spread(w, 0)
                        norm_spread(w, 1)
                    if c == 2:
                        norm_spread(w, 2)
                unit(n + 1, r, 1, early=early, after=after)

            pe.wait_ge(consts, 16 * NCONST)
            for r in range(N_MEMU):
                l, s = r // 4, r % 2
                pe.wait_ge(prepped, r + 1)
                if r >= 2:
                    pe.wait_ge(freed[s], 3 * (r // 2))
                landed = (lambda k: pe.wait_ge(mem_hr, KD * l + k + 1)) if r % 4 == 0 else None
                products(ps[:, 3 * s, 0:N_MEM], lambda k: w_hi[:, s, k * P:(k + 1) * P],
                         lambda k: w_lo[:, s, k * P:(k + 1) * P], lambda k: hm_hi[l][:, k, :],
                         lambda k: hm_lo[l][:, k, :], range(KD), landed=landed).then_inc(proj, 3)
                if r == 0:
                    pe.wait_ge(mem_sum, 1)
                    pe.matmul(ps[0:32, 6, 0:N_MEM], sel[:, SEL_ALL, :], mem_ssq[:, :], start=True, stop=True) \
                        .then_inc(mem_st, 1)
                if r == 1:
                    pe.wait_ge(mem_rs, 1)
                    pe.wait_ge(consts2, 16)
                    pe.matmul(ps[:, 7, 0:N_MEM], sel_t[0:32, SEL_ALL, :], mem_rstd[:, :], start=True, stop=True) \
                        .then_inc(mem_bc, 1)

            def memory_step(u):
                if u == 2:
                    pe.wait_ge(mem_ksq, 4)
                    for t in range(4):
                        mm = pe.matmul(ps[0:32, 7, 0:N_MEM], sel[:, t, :], mk_sq[:, t, :], start=(t == 0),
                                       stop=(t == 3))
                    mm.then_inc(mem_st, 1)
                if u in (3, 4):
                    pe.wait_ge(mem_rs, 2)
                    if u == 4:
                        pe.wait_ge(mem_kn, 2)
                    for t in range(2 * (u - 3), 2 * (u - 3) + 2):
                        pe.matmul(ps[:, 7, (t % 2) * N_MEM:(t % 2 + 1) * N_MEM], sel_t[0:32, t, :], mem_rstd[:, :],
                                  start=True, stop=True).then_inc(mem_bc, 1)
                if u in (5, 6):
                    l = u - 5
                    if u == 5:
                        pe.wait_ge(mem_kn, 4)
                    else:
                        pe.wait_ge(mem_vd, 1)
                    for kc in range(2):
                        for t in range(2):
                            mm = pe.transpose(ps[:, 7, (kc * 2 + t) * P:(kc * 2 + t + 1) * P],
                                              mv_t[:, 2 * l + t, kc * P:(kc + 1) * P], ident[:, :])
                    mm.then_inc(mem_vt, 1)

            def mixer_stats(l, tiles, m, t):
                idx = tiles.index(t)
                pe.wait_ge(m["z_sq"], idx + 1)
                zs = z_sq if l == 0 else z_sq1
                for c in range(NCH):
                    mm = pe.matmul(ps[32 * c:32 * c + 32, 6, 0:CH], sel[:, sel_of(l, t), :],
                                   zs[:, idx % 2, c * CH:(c + 1) * CH], start=(idx == 0),
                                   stop=(idx == len(tiles) - 1), skip_group_check=True)
                mm.then_inc(m["z_stat"], 1)

            def sample_attention(l):
                m = mx[l]
                st_items = sample_items(l)
                for n, (kind, j) in enumerate(st_items):
                    pe.wait_ge(m["qpad_filled"], n + 1)
                    if n == 0:
                        pe.wait_ge(m["caches"], 16 * (5 if l == 0 else 2))
                        if l == 0:
                            pe.wait_ge(m["s_keys"], 1)
                    width = KEYS_S if kind == "swa" else N_MEM
                    keys = s_k if kind == "swa" else s_mk[l]
                    for b in range(DEC_BATCH):
                        for i in range(2):
                            mm = pe.matmul(ps[:, n, 0:width], q_pad[:, b * 256 + i * P:b * 256 + (i + 1) * P],
                                           keys[:, i, b, :], start=(b + i == 0), stop=(b + i == DEC_BATCH))
                    mm.then_inc(m["s_scores"], 1)
                for n, (kind, j) in enumerate(st_items):
                    pe.wait_ge(m["s_normed"], n + 1)
                    if kind == "swa":
                        pe.transpose(ps[:, 4, j * P:(j + 1) * P], s_p[:, n, 0:P], ident[:, :])
                        mm = pe.transpose(ps[0:TS, 5, j * P:(j + 1) * P], s_p[:, n, P:KEYS_S], ident[:, :])
                    else:
                        for kc in range(2):
                            mm = pe.transpose(ps[:, 6, kc * P:(kc + 1) * P], s_p[:, n, kc * P:(kc + 1) * P],
                                              ident[:, :])
                    mm.then_inc(m["s_turned"], 1)
                if l == 0:
                    pe.wait_ge(m["s_turned_taken"], 2)
                    out = ps[:, 7, :].rearrange("p (i j b r) -> p i j b r", i=2, j=4, b=DEC_BATCH)
                    for i in range(2):
                        new = sp_new[:, :, :].rearrange("p j (b r) -> p j b r", r=16)[:, :, :, 8 * i:8 * i + 8]
                        pe.matmul(out[:, i, 0:3], v_tok[0:TS, NB, i * P:(i + 1) * P], new, start=True, stop=False,
                                  skip_group_check=True)
                        for b in range(DEC_BATCH):
                            rhs = sp_t[:, 0:3, b * 16 + 8 * i:b * 16 + 8 * i + 8]
                            mm = pe.matmul(out[:, i, 0:3, b], s_v[:, b, i * P:(i + 1) * P], rhs, start=False,
                                           stop=True, skip_group_check=True)
                    mm.then_inc(m["s_pv"], 1)
                    pe.wait_ge(m["s_turned_taken"], 3)
                else:
                    pe.wait_ge(m["s_turned_taken"], 1)
                out = ps[:, 0, 0:P].rearrange("p (i b r) -> p i b r", i=2, b=DEC_BATCH)
                for i in range(2):
                    for b in range(DEC_BATCH):
                        for kc in range(2):
                            mm = pe.matmul(out[:, i, b], s_mv[l][:, kc, b, i * P:(i + 1) * P],
                                           sp_tm[:, kc, b * 16 + 8 * i:b * 16 + 8 * i + 8],
                                           start=(kc == 0), stop=(kc == 1))
                mm.then_inc(m["s_pv"], 1)

            def prompt_attention(l):
                m = mx[l]
                items = swa_items(l)
                se, pt = (s_exp, p_t) if l == 0 else (s_exp1, p_t1)
                qt = 8 if l == 0 else 12
                N = len(items)
                pe.wait_ge(m["s_pv_taken"], 2 if l == 0 else 1)

                def scores(n):
                    kind, b, g = items[n]
                    if n >= 2:
                        pe.wait_ge(m["ready"], n - 1)
                        if items[n - 2][0] == "mem":
                            pe.wait_ge(m["exped"], n - 1)
                    q0 = TS + b * BLOCK
                    out = banks(2 * (n % 2), 2, 1024)
                    step = 256 if kind == "swa" else 512
                    for hh in range(3 if kind == "swa" else 2):
                        if kind == "swa":
                            i, half = g // 2, g % 2
                            rows = slice(64 * half, 64 * half + 64)
                            k0 = max(TS + (b - 1) * BLOCK, TS)
                            w = BLOCK if b == 0 else 256
                            lhs, rhs = z[rows, 3 * i + hh, q0:q0 + BLOCK], z[rows, 6 + i, k0:k0 + w]
                        else:
                            rows, w = slice(64 * hh, 64 * hh + 64), 256
                            lhs, rhs = z[rows, qt + g, q0:q0 + BLOCK], mem_k[rows, 2 * l + g, :]
                        mm = pe.matmul(out[:, hh * step:hh * step + w], lhs, rhs, start=True, stop=True)
                    mm.then_inc(m["scored"], 1)

                def turn(n):
                    kind, b, g = items[n]
                    nh = 3 if kind == "swa" else 2
                    pe.wait_ge(m["normed"], n + 1)
                    if n >= 1:
                        pe.wait_ge(m["pturned_taken"], n)
                    out = banks(4, 2, 768)
                    for kc in range(1 if kind == "swa" and b == 0 else 2):
                        for hh in range(nh):
                            at = (kc * nh + hh) * P
                            k0 = hh * 256 + kc * P
                            mm = pe.transpose(out[:, at:at + P], se[:, n % RING, k0:k0 + P],
                                              ident[:, :])
                    mm.then_inc(m["pturned"], 1)

                def values(n):
                    kind, b, g = items[n]
                    pe.wait_ge(m["pturned_taken"], n + 1)
                    if n >= 2:
                        pe.wait_ge(m["o_done"], n - 1)
                    if kind == "swa":
                        half = g % 2
                        kcs = [0] if b == 0 else [0, 1]
                        for kc in kcs:
                            mm = pe.matmul(ps[64 * half:64 * half + 64, 6 + n % 2, 0:384],
                                           v_tok[:, b - len(kcs) + 1 + kc, g * HD:(g + 1) * HD],
                                           pt[:, n % 2, kc * 384:(kc + 1) * 384], start=(kc == 0), stop=(kc == kcs[-1]))
                    else:
                        for half in range(2):
                            for kc in range(2):
                                mm = pe.matmul(ps[64 * half:64 * half + 64, 6 + n % 2, 0:P],
                                               mem_v[:, l, kc, (2 * g + half) * HD:(2 * g + half + 1) * HD],
                                               pt[:, n % 2, kc * 256 + half * P:kc * 256 + (half + 1) * P],
                                               start=(kc == 0), stop=(kc == 1))
                    mm.then_inc(m["pv"], 1)

                for n in range(N + LAG + 1):
                    if n < N:
                        scores(n)
                    if 0 <= n - LAG < N:
                        turn(n - LAG)
                    if 0 <= n - LAG - 1 < N:
                        values(n - LAG - 1)

            def gate():
                m = mx[1]
                tiles = [("s", 0)] + [("p", b) for b in range(NB)]
                pe.wait_ge(m["masked"], 2)
                for n in range(NB + 2):
                    if n < NB + 1:
                        kind, b = tiles[n]
                        w = TS if kind == "s" else BLOCK
                        t0 = 0 if kind == "s" else TS + b * BLOCK
                        if n >= 1:
                            pe.wait_ge(m["gate_taken"], n)
                        out = banks(0, 2, 768)
                        for t in range(6):
                            mm = pe.transpose(out[0:w, t * P:(t + 1) * P], z[:, 6 + t, t0:t0 + w], ident[:, :])
                        mm.then_inc(m["gate_turned"], 1)
                    if n >= 1:
                        q = n - 1
                        kind, b = tiles[q]
                        w = TS if kind == "s" else BLOCK
                        pe.wait_ge(m["gate_taken"], q + 1)
                        if q >= 2:
                            pe.wait_ge(m["gate_biased"], q - 1)
                        out = banks(2 + 2 * (q % 2), 2, 768)
                        ww = ws4 if kind == "s" else ws_t
                        for t in range(6):
                            for half in range(2):
                                grp = (2 * t + half) // 3
                                f0 = t * P + 64 * half
                                if (2 * t) // 3 == (2 * t + 1) // 3:
                                    if half == 0:
                                        mm = pe.matmul(out[:, t * P:t * P + w], vn_tok[0:w, q % 2, f0:f0 + P],
                                                       ww[:, grp, :], start=True, stop=True)
                                else:
                                    mm = pe.matmul(out[64 * half:64 * half + 64, t * P:t * P + w],
                                                   vn_tok[0:w, q % 2, f0:f0 + 64], ww[:, grp, :], start=True, stop=True)
                        mm.then_inc(m["gate_mixed"], 1)

            for l in range(2):
                m = mx[l]
                s0, r0, nu = (S_INA, R_INA, IN_A) if l == 0 else (S_INB, R_INB, IN_B)
                tiles = stat_tiles(l)
                first_units(2 * l, s0, r0 // 2)
                for u in range(2, nu):
                    def after(c):
                        q = NCH * (u - (IN_B - 3)) + c
                        s_i, _, bank, need, _ = spread_b(q)
                        pe.wait_ge(m["z_rstd"], 1)
                        if need is not None:
                            pe.wait_ge(m["z_normed"], need)
                        pe.matmul(ps[:, bank, 0:CH], sel_t[32 * c:32 * c + 32, s_i, :], rstd[32 * c:32 * c + 32, :],
                                  start=True, stop=True).then_inc(m["z_spread"], 1)
                    unit(s0 + u, (r0 + u) // 2, u % 2, after=after if l == 1 and u >= IN_B - 3 else None)
                    if u - 2 < len(tiles):
                        mixer_stats(l, tiles, m, tiles[u - 2])
                    if l == 0:
                        memory_step(u)
                if l == 0:
                    for q in range(5):
                        if q == 0:
                            pe.wait_ge(freed[0], 3 * ((R_INA + IN_A) // 2))
                            pe.wait_ge(freed[1], 3 * ((R_INA + IN_A) // 2))
                        if q >= 2:
                            pe.wait_ge(m["turned_taken"], q - 1)
                        bank = 7 if q % 2 == 0 else 0
                        for b in ([2 * q, 2 * q + 1] if q < 4 else [8]):
                            w, t0 = (BLOCK, TS + b * BLOCK) if b < 8 else (TS, 0)
                            for t in range(2):
                                at = ((b % 2) * 2 + t) * P
                                mm = pe.transpose(ps[0:w, bank, at:at + P], z[:, 10 + t, t0:t0 + w], ident[:, :])
                        mm.then_inc(m["turned"], 1)
                if l == 0:
                    pe.wait_ge(m["z_rstd"], 1)
                    for s_i, c, bank, need in spreads_a():
                        if need is not None:
                            pe.wait_ge(m["z_normed"], need)
                        pe.matmul(ps[:, bank, 0:CH], sel_t[32 * c:32 * c + 32, s_i, :], rstd[32 * c:32 * c + 32, :],
                                  start=True, stop=True).then_inc(m["z_spread"], 1)
                else:
                    pe.wait_ge(freed[0], 3 * ((R_INB + IN_B) // 2))
                    pe.wait_ge(freed[1], 3 * ((R_INB + IN_B) // 2))
                    pe.wait_ge(m["z_normed"], 24)
                    gate()
                if l == 0:
                    pe.wait_ge(m["z_normed"], 30)
                    pe.wait_ge(m["turned_taken"], 5)
                    for t in range(2):
                        mm = pe.transpose(ps[0:TS, 7, t * P:(t + 1) * P], z[:, 6 + t, 0:TS], ident[:, :])
                    mm.then_inc(m["turned"], 1)
                    pe.wait_ge(m["turned_taken"], 6)
                sample_attention(l)
                if l == 1:
                    pe.wait_ge(m["gate_biased"], NB + 1)
                prompt_attention(l)
                s0, r0 = (S_OUTA, R_OUTA) if l == 0 else (S_OUTB, R_OUTB)
                pe.wait_ge(m["o_done"], len(swa_items(l)))
                pe.wait_ge(m["s_done"], 1)
                if l == 1:
                    pe.wait_ge(m["gate_done"], NB + 1)
                with pe.Fori(0, OUT_U // 2) as i:
                    for s in range(2):
                        unit(2 * i + s0 + s, i + r0 // 2, s)
                s0, r0 = S_FFN[l], R_FFN[l]
                first_units(2 * l + 1, s0, r0 // 2)

                def down(n, grp):
                    pe.wait_ge(prepped, n + 2)
                    for q in range(KD * NCH):
                        oo, c = q // NCH, q % NCH
                        if q == 0:
                            pe.wait_ge(g_done[l], 6 * grp + 6)
                        if q >= 5:
                            pe.wait_ge(dn_added, 24 * (NG * l + grp) + q - 4)
                        elif q == 0:
                            pe.wait_ge(freed[1], 3 * (r0 // 2) + 6 * grp + 6)
                        t0 = c * CH
                        for f in range(2):
                            mm = products(ps[:, 3 + (q + 1) % 5, 0:CH],
                                          lambda k: d_hi[:, f, oo * P:(oo + 1) * P],
                                          lambda k: d_lo[:, f, oo * P:(oo + 1) * P],
                                          lambda k: g_hi[:, f, t0:t0 + CH], lambda k: g_lo[:, f, t0:t0 + CH],
                                          [0], first=(f == 0), last=(f == 1))
                        mm.then_inc(dn_done, 1)

                def group(grp, last, first=False):
                    n = 6 * grp + (s0 + 1)
                    r = 2 * grp + r0 // 2
                    prev = 24 * (NG * l + grp)
                    early = None if first else (lambda c: pe.wait_ge(dn_added, prev - 4 + c))
                    if not first:
                        unit(n, r, 1, early=early)
                    unit(n + 1, r + 1, 0)
                    unit(n + 2, r + 1, 1)
                    if not last:
                        unit(n + 3, r + 2, 0)
                    down(n + (3 if last else 4), grp)

                group(0, False, first=True)
                with pe.Fori(1, NG - 1) as i:
                    group(i, False)
                group(NG - 1, True)

        @block.scalar
        def _(act):
            def scopy(out, in_):
                return act.activation(out, in_, ACT.Copy)

            act.dma_start(mem_x[:, :, :], d["mem_t"]).then_inc(mem_landed, 16)
            for name, t in CONST_LOADS:
                act.dma_start(t[:], d[name]).then_inc(consts, 16)
            act.dma_start(sel_t[:, :, :], d["sel_t"]).then_inc(consts2, 16)

            def load_x(j):
                act.dma_start(x[:, 2 * j:2 * j + 2, :], d["x_t"][:, 2 * j:2 * j + 2, :]).then_inc(x_landed[j], 16)

            load_x(0)

            def high_of_unit(n, slot, dst, free=None, turn=None):
                act.wait_ge(raw_landed[slot], 16 * (n // 2 + 1 if turn is None else turn))
                if free is not None:
                    act.wait_ge(*free)
                if turn is not None:
                    act.wait_ge(consts, 16 * NCONST)
                scopy(dst, raw[:, slot]).then_inc(hi_cut, 1)

            def high_up(n, r):
                high_of_unit(n, n % 2, w_hi[:, r % 2], (proj, 3 * (r - 1)) if r >= 2 else None)


            def square(w, e):
                oo, c = e // NCH, e % NCH
                src = x[:, oo, c * CH:(c + 1) * CH]
                if oo == 0:
                    if w >= 1:
                        act.wait_ge(ssq_sum, w)
                    act.activation(ssq[:, c * CH:(c + 1) * CH], src, ACT.Square).then_inc(squared, 1)
                else:
                    p = e - NCH
                    if N_SSQ * w + p >= 4:
                        need = N_SSQ * w + p - 3 if p >= 4 else N_SSQ * w
                        act.wait_ge(ssq_added, need)
                    act.activation(sq_ring[:, p % 4], src, ACT.Square).then_inc(squared, 1)

            def norm_root(w, n, r):
                act.wait_ge(ssq_sum, w + 1)
                act.wait_ge(outs, 16 * n_out[0])
                act.activation(root[:, :], ps[0:96, 7, 0:CH], ACT.Sqrt, bias=cols[0:96, 0:1],
                               scale=1.0 / D_MODEL).then_inc(rooted, 1)
                high_up(n, r)
                for c in range(NCH):
                    act.wait_ge(spread, NCH * w + c + 1)
                    scopy(rb[:, c * CH:(c + 1) * CH], ps[:, 6 + c % 2, 0:CH]).then_inc(rb_taken, 1)

            def high_of_h(w, e):
                c, k = piece(w, e)
                g_i = (0, 2, 1, 3)[w]
                cs = slice(c * CH, (c + 1) * CH)
                act.activation(h_hi[:, k, cs], x[:, k, cs], ACT.Copy, scale=gain[:, g_i, k:k + 1]) \
                    .then_inc(h_cut, 1)

            for n in range(2):
                high_up(n, n)
            load_x(1)
            act.wait_ge(mem_landed, 16)
            act.wait_ge(consts, 16 * NCONST)
            for l in range(2):
                for k in range(KD):
                    act.activation(hm_hi[l][:, k, :], mem_x[:, k, :], ACT.Copy, scale=gain[:, 4 + l, k:k + 1]) \
                        .then_inc(mem_hc, 1)
                if l == 0:
                    act.activation(mem_sq[:, :, :], mem_x[:, :, :], ACT.Square).then_inc(mem_sqd, 1)
                    load_x(2)
            load_x(3)
            for r in range(N_MEMU):
                if r == 0:
                    act.wait_ge(mem_st, 1)
                    act.activation(mem_root_t[:, :], ps[0:32, 6, 0:N_MEM], ACT.Sqrt, bias=cols[0:32, 0:1],
                                   scale=1.0 / D_MODEL).then_inc(mem_root, 1)
                high_up(r + 2, r + 2)
                if r == 0:
                    act.wait_ge(mem_bc, 1)
                    scopy(mem_rb[:, :], ps[:, 7, 0:N_MEM]).then_inc(mem_rbt, 1)
                for e in range(X_PIECES[r], X_PIECES[r + 1]):
                    if e % 6 == 0:
                        act.wait_ge(x_landed[e // 6], 16)
                    high_of_h(0, e)
                for e in range(X_PIECES[r], X_PIECES[r + 1]):
                    square(0, e)
            act.wait_ge(freed[0], 12)
            act.wait_ge(freed[1], 12)
            act.dma_start(o["mem_v"], mv_t[:, :, :]).then_inc(mem_stored, 16)
            for t in range(4):
                act.activation(mk_sq[:, t, :], mk_raw[:, t, :], ACT.Square).then_inc(mem_ksq, 1)

            act.dma_start(o["win_k_s"][:, 0:BLOCK - DEC_SEQ], d["cache_k"][:, DEC_SEQ:BLOCK]).then_inc(outs, 16)
            act.dma_start(o["win_v_s"][:, 0:BLOCK - DEC_SEQ], d["cache_v"][:, DEC_SEQ:BLOCK]).then_inc(outs, 16)
            n_out[0] += 2

            def memory_step(u):
                if u == 2:
                    act.wait_ge(mem_st, 2)
                    act.activation(mem_root_t[:, :], ps[0:32, 7, 0:N_MEM], ACT.Sqrt, bias=cols[0:32, 0:1],
                                   scale=1.0 / HD).then_inc(mem_root, 1)
                if u in (5, 6):
                    l = u - 5
                    act.wait_ge(mem_vt, l + 1)
                    scopy(mem_v[:, l, :, :], ps[:, 7, :].rearrange("p (k f) -> p k f", k=2)).then_inc(mem_vd, 1)
                if u == 6:
                    act.wait_ge(mem_kn, 4)
                    act.dma_start(o["mem_k"], mem_k[:, :, :]).then_inc(outs, 16)
                    n_out[0] += 1

            def sample_attention(l):
                m = mx[l]
                ss = s_stat if l == 0 else s_stat1
                items = sample_items(l)
                for n, (kind, j) in enumerate(items):
                    act.wait_ge(m["s_max"], n + 1)
                    src = s_p[:, n, 0:KEYS_S] if kind == "swa" else ps[:, n, 0:N_MEM]
                    width = KEYS_S if kind == "swa" else N_MEM
                    ins = act.activation(s_p[:, n, 0:width], src, ACT.Exp, bias=ss[:, 1, n:n + 1],
                                         accum_out=ss[:, 2, n:n + 1])
                    if kind == "swa":
                        ins = act.activation(ss[:, 4, n:n + 1], ss[:, 3, n:n + 1], ACT.Exp)
                    ins.then_inc(m["s_exped"], 1)
                if l == 0:
                    act.wait_ge(m["s_turned"], 3)
                    scopy(sp_t[:, 0:3, :], ps[:, 4, 0:384].rearrange("p (j n) -> p j n", j=3)) \
                        .then_inc(m["s_turned_taken"], 1)
                    scopy(sp_new[:, :, :], ps[0:TS, 5, 0:384].rearrange("p (j n) -> p j n", j=3)) \
                        .then_inc(m["s_turned_taken"], 1)
                act.wait_ge(m["s_turned"], len(items))
                scopy(sp_tm, ps[:, 6, 0:256].rearrange("p (k n) -> p k n", k=2)).then_inc(m["s_turned_taken"], 1)
                act.wait_ge(m["s_pv_taken"], 2 if l == 0 else 1)
                t0 = 0 if l == 0 else 6
                oo = o_s if l == 0 else o_s1
                scopy(h_hi[:, t0:8, 0:TS], oo[:, t0:8, :]).then_inc(m["s_cut"], 1)

            def prompt_attention(l):
                m = mx[l]
                items = swa_items(l)
                se, pt, st = (s_exp, p_t, stat) if l == 0 else (s_exp1, p_t1, stat1)
                N = len(items)
                if l == 0:
                    act.wait_ge(outs, 16 * n_out[0])

                def exps(n):
                    kind, b, g = items[n]
                    act.wait_ge(m["ready"], n + 1)
                    if kind == "mem" and n >= RING:
                        act.wait_ge(m["pturned"], n - RING + 1)
                    w = BLOCK if kind == "swa" and b == 0 else 256
                    for hh in range(3 if kind == "swa" else 2):
                        dst = se[:, n % RING, hh * 256:hh * 256 + w]
                        src = dst if kind == "swa" else ps[:, 2 * (n % 2) + hh, 0:w]
                        ins = act.activation(dst, src, ACT.Exp, bias=st[:, n % 4, 1, hh:hh + 1],
                                             accum_out=st[:, n % 4, 2, hh:hh + 1])
                    if kind == "swa":
                        ins = act.activation(st[:, n % 4, 4, :], st[:, n % 4, 3, :], ACT.Exp)
                    ins.then_inc(m["exped"], 1)

                def take(n):
                    kind, b, g = items[n]
                    nh = 3 if kind == "swa" else 2
                    w = nh * P * (1 if kind == "swa" and b == 0 else 2)
                    act.wait_ge(m["pturned"], n + 1)
                    if n >= 2:
                        act.wait_ge(m["pv"], n - 1)
                    scopy(pt[:, n % 2, 0:w], banks(4, 2, 768)[:, 0:w]).then_inc(m["pturned_taken"], 1)

                def high(n):
                    act.wait_ge(m["pv"], n + 1)
                    dst, src = o_view(items[n], n, h_hi)
                    scopy(dst, src).then_inc(m["o_cut"], 1)

                for n in range(N + LAG + 2):
                    if 0 <= n - LAG < N:
                        take(n - LAG)
                    if 0 <= n - LAG - 1 < N:
                        high(n - LAG - 1)
                    if n < N:
                        exps(n)
                    if l == 1 and n < NB + 1:
                        w, t0 = (TS, 0) if n == 0 else (BLOCK, TS + (n - 1) * BLOCK)
                        act.wait_ge(m["gate_mult"], n + 1)
                        scopy(h_hi[:, 0:6, t0:t0 + w], z[:, 0:6, t0:t0 + w]).then_inc(m["gate_cut"], 1)

            def ffn(l):
                r0 = R_FFN[l]

                def tap2(f, r, s, wide):
                    ab = a_buf[:, s]
                    act.wait_ge(freed[0], 3 * r + 3)
                    if wide:
                        act.wait_ge(freed[1], 3 * r - 3)
                    act.wait_ge(consts, 16 * NCONST)
                    cc = conv_c[:, l, bass.ds(f, 1), :].rearrange("p o c -> p (o c)")
                    act.activation(c_buf[:, s, TS:T], ab[:, 50:50 + SEQ], ACT.Identity, bias=cc[:, 3:4],
                                   scale=cc[:, 2:3])
                    act.activation(c_buf[:, s, 0:TS].rearrange("p (b t) -> p b t", b=DEC_BATCH),
                                   ab[:, 0:48].rearrange("p (b t) -> p b t", b=DEC_BATCH)[:, :, 2:6], ACT.Identity,
                                   bias=cc[:, 3:4], scale=cc[:, 2:3]).then_inc(c0_done[l], 1)

                def silu(f, s):
                    act.wait_ge(conv_done[l], f + 1)
                    act.wait_ge(consts, 16 * NCONST)
                    act.activation(c_buf[:, s], c_buf[:, s], ACT.Silu).then_inc(silued[l], 1)

                def high(f, r, s, dn):
                    for c in range(NCH):
                        act.wait_ge(freed[1], 3 * r + c + 1)
                        if c == 0 and dn is not None:
                            act.wait_ge(dn_done, dn)
                        act.wait_ge(consts, 16 * NCONST)
                        scopy(g_hi[:, s, c * CH:(c + 1) * CH], g_f[:, c * CH:(c + 1) * CH]).then_inc(g_cut[l], 1)

                h = r0 // 2
                n0 = S_FFN[l]
                tap2(0, h, 0, False)

                def up(i, j, ring, before):
                    n = n0 + j
                    high_of_unit(None, n % 2, w_hi[:, ring % 2], (proj, 12 * i + 3 * (r0 + before + 1)),
                                 turn=3 * i + n // 2 + 1)

                def down(i, j, q):
                    n = n0 + j
                    high_of_unit(None, n % 2, d_hi[:, q], None, turn=3 * i + n // 2 + 1)

                def group(i, last, first=False):
                    f = 2 * i
                    r = 2 * i + h
                    dn = None if first and l == 0 else 24 * i + 24 * NG * l
                    silu(f, 0)
                    high(f, r, 0, dn)
                    up(i, 3, 3, 1)
                    if last:
                        down(i, 4, 0)
                        tap2(f + 1, r + 1, 1, not first)
                        down(i, 5, 1)
                    else:
                        tap2(f + 1, r + 1, 1, not first)
                        up(i, 4, 4, 2)
                        down(i, 5, 0)
                        down(i, 6, 1)
                    silu(f + 1, 1)
                    high(f + 1, r + 1, 1, None)
                    if not last:
                        up(i, 7, 5, 3)
                        up(i, 8, 6, 4)
                        tap2(f + 2, r + 2, 0, True)

                group(0, False, first=True)
                with act.Fori(1, NG - 1) as i:
                    group(i, False)
                group(NG - 1, True)

            for l in range(2):
                m = mx[l]
                tiles = stat_tiles(l)
                nu, r0 = (IN_A, R_INA) if l == 0 else (IN_B, R_INB)
                zs = z_sq if l == 0 else z_sq1
                norm_root(2 * l, (S_INA, S_INB)[l] + 2, r0 + 2)
                if l == 1:
                    for name, t in (("ws_t", ws_t), ("ws4", ws4), ("bb", bb), ("bb4", bb4)):
                        act.dma_start(t[:, :, :], d[name]).then_inc(m["gate_in"], 16)
                for u in range(nu):
                    r = r0 + u
                    if u >= 1:
                        high_up((S_INA, S_INB)[l] + u + 2, r + 2)
                    t = unit_tiles(l)[u]
                    act.wait_ge(freed[u % 2], 3 * (r // 2) + 3)
                    if l == 1 and t < 12:
                        act.activation(z[:, t, :], z[:, t, :], ACT.Gelu).then_inc(m["gelud"], 1)
                    if t in tiles:
                        if l == 1 and t < 12:
                            act.wait_ge(m["gelud"], u - 1)
                        if u >= 2:
                            act.wait_ge(m["z_stat"], u - 1)
                        act.activation(zs[:, u % 2, :], z[:, t, :], ACT.Square).then_inc(m["z_sq"], 1)
                    if l == 0:
                        memory_step(u)
                    if u == len(tiles) + 1:
                        act.wait_ge(m["z_stat"], len(tiles))
                        act.activation(root[:, :], ps[0:96, 6, 0:CH], ACT.Sqrt, bias=cols[0:96, 0:1],
                                       scale=cols[0:96, 1 + l:2 + l]).then_inc(m["z_root"], 1)
                act.wait_ge(proj, 3 * (r0 + nu))
                if l == 0:
                    for i in range(2):
                        act.dma_start(s_k[:, i, :, 0:BLOCK], d["s_k"][:, i]).then_inc(m["caches"], 16)
                act.dma_start(s_mk[l][:, :, :, :], d["s_mk"][l]).then_inc(m["caches"], 16)
                act.dma_start(s_mv[l][:, :, :, :], d["s_mv"][l]).then_inc(m["caches"], 16)
                if l == 0:
                    act.dma_start(s_v[:, :, :], d["s_v"]).then_inc(m["caches"], 16)
                    for q in range(5):
                        act.wait_ge(m["turned"], q + 1)
                        bank = 7 if q % 2 == 0 else 0
                        if q < 4:
                            scopy(v_tok[:, 2 * q:2 * q + 2, :].rearrange("p b n -> p (b n)"), ps[:, bank, :]) \
                                .then_inc(m["turned_taken"], 1)
                        else:
                            scopy(v_tok[0:TS, NB, :], ps[0:TS, bank, 0:256]).then_inc(m["turned_taken"], 1)
                    act.wait_ge(m["turned"], 6)
                    scopy(k_tok[:, :], ps[0:TS, 7, 0:256]).then_inc(m["turned_taken"], 1)
                    act.wait_ge(m["turned_taken"], 6)
                    for b in range(DEC_BATCH):
                        rows = slice(DEC_SEQ * b, DEC_SEQ * (b + 1))
                        act.dma_start(o["win_k_s"][b, BLOCK - DEC_SEQ:BLOCK], k_tok[rows, :]).then_inc(outs, 16)
                        act.dma_start(o["win_v_s"][b, BLOCK - DEC_SEQ:BLOCK], v_tok[rows, NB, :]).then_inc(outs, 16)
                    act.dma_start(o["win_k_p"], z[:, 6:8, T - BLOCK:T]).then_inc(outs, 16)
                    act.dma_start(o["win_v_p"], z[:, 10:12, T - BLOCK:T]).then_inc(outs, 16)
                    n_out[0] += 2 * DEC_BATCH + 2
                else:
                    act.wait_ge(m["z_normed"], 24)
                    act.dma_start(o["chunk_p"], z[:, 6:12, T - BLOCK:T]).then_inc(outs, 16)
                    act.dma_start(o["chunk_s"], z[:, 6:12, 0:TS]).then_inc(outs, 16)
                    n_out[0] += 2
                if l == 1:
                    for n in range(NB + 1):
                        w = TS if n == 0 else BLOCK
                        act.wait_ge(m["gate_turned"], n + 1)
                        if n >= 2:
                            act.wait_ge(m["gate_mixed"], n - 1)
                        scopy(vn_tok[0:w, n % 2, :], banks(0, 2, 768)[0:w]).then_inc(m["gate_taken"], 1)
                sample_attention(l)
                prompt_attention(l)
                if l == 1:
                    act.wait_ge(conv_done[0], NF)
                    act.wait_ge(state_stored, 16)
                act.dma_start(state_in[:, :, :], d["state"][l]).then_inc(state_landed, 16)
                w = 2 * l + 1
                s0, r0 = (S_OUTA, R_OUTA) if l == 0 else (S_OUTB, R_OUTB)
                for oo in range(KD - 1):
                    high_up(s0 + oo + 2 if oo + 2 < OUT_U else S_FFN[l] + oo + 2 - OUT_U, r0 + oo + 2)
                    for c in range(NCH):
                        act.wait_ge(freed[oo % 2], 3 * ((r0 + oo) // 2) + c + 1)
                        square(w, NCH * oo + c)
                for c in range(NCH):
                    act.wait_ge(proj, 3 * (r0 + KD - 1) + c + 1)
                    for k in range(KD):
                        if k == KD - 1:
                            act.wait_ge(freed[1], 3 * ((r0 + KD - 1) // 2) + c + 1)
                        high_of_h(w, KD * c + k)
                    square(w, NCH * (KD - 1) + c)
                high_up(S_FFN[l] + 1, R_FFN[l] + 1)
                norm_root(w, S_FFN[l] + 2, R_FFN[l] + 2)
                ffn(l)
                if l == 0:
                    high_up(S_INB, R_INB)
                    high_up(S_INB + 1, R_INB + 1)
                    for e in range(KD * NCH):
                        act.wait_ge(dn_added, 24 * (NG - 1) + e + 1)
                        if e % NCH == 0:
                            high_of_h(2, e // NCH)
                        square(2, e)
                    for e in range(KD, KD * NCH):
                        high_of_h(2, e)
                act.wait_ge(st_copied, NF * (l + 1))
                act.dma_start(o["state"][l], state_out[:, :, :]).then_inc(state_stored, 16)
            for oo in range(KD):
                act.wait_ge(dn_added, 24 * (2 * NG - 1) + 3 * (oo + 1))
                act.dma_start(o["y"][:, oo], x[:, oo]).then_inc(outs, 16)
                n_out[0] += 1
            act.wait_ge(outs, 16 * n_out[0])
            act.wait_ge(state_stored, 32)

        @block.vector
        def _(dve):
            TT, TSC, STT = dve.tensor_tensor, dve.tensor_scalar, dve.scalar_tensor_tensor
            dve.wait_ge(consts, 16 * NCONST)
            TSC(nsink_p[:, :], sink_p[:, :], -1.0, None, ALU.mult).then_inc(neg, 1)
            TSC(nsink_s[:, :], sink_s[:, :], -1.0, None, ALU.mult).then_inc(neg, 1)
            TSC(qgain[:, 0:1], hgain[:, 0:1], HD ** -0.5, None, ALU.mult).then_inc(neg, 1)
            TSC(qgain[:, 1:3], hgain[:, 2:4], HD ** -0.5, None, ALU.mult).then_inc(neg, 1)

            dve.wait_ge(neg, 4)

            def low_of_h(w, e):
                c, k = piece(w, e)
                g_i = (0, 2, 1, 3)[w]
                cs = slice(c * CH, (c + 1) * CH)
                dve.wait_ge(h_cut, KD * NCH * w + e + 1)
                STT(out=h_lo[:, k, cs], in0=x[:, k, cs], scalar=gain[:, g_i, k:k + 1], in1=h_hi[:, k, cs].bitcast(F32),
                    op0=ALU.mult, op1=ALU.subtract).then_inc(h_ready, 1)

            def norm_rstd(w):
                dve.wait_ge(rooted, w + 1)
                dve.reciprocal(rstd[:, :], root[:, :]).then_inc(recip, 1)

            for l in range(2):
                for k in range(KD):
                    dve.wait_ge(mem_hc, KD * l + k + 1)
                    STT(out=hm_lo[l][:, k, :], in0=mem_x[:, k, :], scalar=gain[:, 4 + l, k:k + 1],
                        in1=hm_hi[l][:, k, :].bitcast(F32), op0=ALU.mult, op1=ALU.subtract).then_inc(mem_hr, 1)
                if l == 0:
                    dve.wait_ge(mem_sqd, 1)
                    dve.tensor_reduce(mem_ssq[:, :], mem_sq[:, :, :].rearrange("p k t -> p t k"), AX, ALU.add) \
                        .then_inc(mem_sum, 1)
            def add_square(p):
                c = p % NCH
                dve.wait_ge(squared, NCH + p + 1)
                if p >= NCH:
                    dve.wait_ge(ssq_added, p - 2)
                ch = ssq[:, c * CH:(c + 1) * CH]
                TT(ch, ch, sq_ring[:, p % 4], ALU.add).then_inc(ssq_added, 1)

            dve.wait_ge(mem_root, 1)
            dve.reciprocal(mem_rstd[:, :], mem_root_t[:, :]).then_inc(mem_rs, 1)
            dve.wait_ge(mem_rbt, 1)
            for r in range(N_MEMU):
                l, q = r // 4, r % 4
                dve.wait_ge(proj, 3 * (r + 1))
                dst = mk_raw if q < 2 else mv_t
                TT(dst[:, 2 * l + q % 2, :], ps[:, 3 * (r % 2), 0:N_MEM], mem_rb[:, :], ALU.mult) \
                    .then_inc(freed[r % 2], 3)
                for e in range(X_PIECES[r], X_PIECES[r + 1]):
                    low_of_h(0, e)
                for e in range(max(NCH, X_PIECES[r]), X_PIECES[r + 1]):
                    add_square(e - NCH)

            def memory_step(u):
                if u == 2:
                    dve.wait_ge(mem_root, 2)
                    dve.reciprocal(mem_rstd[:, :], mem_root_t[:, :]).then_inc(mem_rs, 1)
                if u in (3, 4):
                    dve.wait_ge(mem_bc, 2 * (u - 3) + 3)
                    for t in range(2 * (u - 3), 2 * (u - 3) + 2):
                        STT(out=mem_k[:, t, :], in0=mk_raw[:, t, :], scalar=hgain[:, 4 + t // 2:5 + t // 2],
                            in1=ps[:, 7, (t % 2) * N_MEM:(t % 2 + 1) * N_MEM], op0=ALU.mult, op1=ALU.mult) \
                            .then_inc(mem_kn, 1)

            def sample_attention(l):
                m = mx[l]
                ss, oo = (s_stat, o_s) if l == 0 else (s_stat1, o_s1)
                items = sample_items(l)
                qv = q_pad[:, :].rearrange("p (b s) -> p b s", b=DEC_BATCH)
                if l == 0:
                    dve.wait_ge(proj, 3 * (R_INA + IN_A))
                    for i in range(2):
                        ins = dve.tensor_copy(s_k[:, i, :, BLOCK:KEYS_S],
                                              z[:, 6 + i, 0:TS][:, None, :].to_broadcast([P, DEC_BATCH, TS]))
                    ins.then_inc(m["s_keys"], 1)
                dve.wait_ge(m["qpad_zeroed"], 1)

                def fill(n):
                    kind, j = items[n]
                    if n >= 1:
                        dve.wait_ge(m["s_scores"], n)
                    for i in range(2):
                        for half in range(2):
                            rows = slice(64 * half, 64 * half + 64)
                            at = i * P + (2 * i + half) * DEC_SEQ
                            t = 3 * i + j if kind == "swa" else (8 if l == 0 else 12) + i
                            ins = dve.tensor_copy(qv[rows, :, at:at + DEC_SEQ],
                                                  z[rows, t, 0:TS].rearrange("p (b t) -> p b t", b=DEC_BATCH))
                    ins.then_inc(m["qpad_filled"], 1)

                def top(n):
                    kind, j = items[n]
                    dve.wait_ge(m["s_scores"], n + 1)
                    if kind == "swa":
                        STT(out=s_p[:, n, 0:KEYS_S], in0=nd_s[:, :], scalar=cols[:, 3 + j:4 + j],
                            in1=ps[:, n, 0:KEYS_S], op0=ALU.mult, op1=ALU.add).then_inc(m["s_biased"], 1)
                        dve.wait_ge(m["s_biased"], 3 * n + 1)
                        dve.tensor_reduce(ss[:, 0, n:n + 1], s_p[:, n, 0:KEYS_S], AX, ALU.max, negate=True) \
                            .then_inc(m["s_biased"], 1)
                        dve.wait_ge(m["s_biased"], 3 * n + 2)
                        TT(ss[:, 1, n:n + 1], ss[:, 0, n:n + 1], nsink_s[:, j:j + 1], ALU.min) \
                            .then_inc(m["s_biased"], 1)
                        dve.wait_ge(m["s_biased"], 3 * n + 3)
                        TT(ss[:, 3, n:n + 1], ss[:, 1, n:n + 1], nsink_s[:, j:j + 1], ALU.subtract) \
                            .then_inc(m["s_max"], 1)
                    else:
                        dve.tensor_reduce(ss[:, 1, n:n + 1], ps[:, n, 0:N_MEM], AX, ALU.max, negate=True) \
                            .then_inc(m["s_max"], 1)

                def scale(n):
                    kind, j = items[n]
                    width = KEYS_S if kind == "swa" else N_MEM
                    dve.wait_ge(m["s_exped"], n + 1)
                    if kind == "swa":
                        TT(ss[:, 0, n:n + 1], ss[:, 2, n:n + 1], ss[:, 4, n:n + 1], ALU.add).then_inc(m["s_recip"], 1)
                        dve.wait_ge(m["s_recip"], 2 * n + 1)
                        dve.reciprocal(ss[:, 5, n:n + 1], ss[:, 0, n:n + 1]).then_inc(m["s_recip"], 1)
                        dve.wait_ge(m["s_recip"], 2 * n + 2)
                    else:
                        dve.reciprocal(ss[:, 5, n:n + 1], ss[:, 2, n:n + 1]).then_inc(m["s_recip"], 1)
                        dve.wait_ge(m["s_recip"], 2 * n + 1)
                    TSC(s_p[:, n, 0:width], s_p[:, n, 0:width], ss[:, 5, n:n + 1], None, ALU.mult) \
                        .then_inc(m["s_normed"], 1)

                N = len(items)
                fill(0)
                for n in range(N + 1):
                    if n + 1 < N:
                        fill(n + 1)
                    if n < N:
                        top(n)
                    if n >= 1:
                        scale(n - 1)
                if l == 0:
                    dve.wait_ge(m["s_pv"], 1)
                    out = ps[:, 7, :].rearrange("p (i j b r) -> p i j b r", i=2, j=4, b=DEC_BATCH)
                    for i in range(2):
                        for half in range(2):
                            rows = slice(64 * half, 64 * half + 64)
                            for j in range(3):
                                ins = dve.tensor_copy(oo[rows, 3 * i + j, :].rearrange("p (b t) -> p b t", b=DEC_BATCH),
                                                      out[rows, i, j, :, 4 * half:4 * half + 4])
                    ins.then_inc(m["s_pv_taken"], 1)
                dve.wait_ge(m["s_pv"], 2 if l == 0 else 1)
                out = ps[:, 0, 0:P].rearrange("p (i b r) -> p i b r", i=2, b=DEC_BATCH)
                for i in range(2):
                    for half in range(2):
                        rows = slice(64 * half, 64 * half + 64)
                        ins = dve.tensor_copy(oo[rows, 6 + i, :].rearrange("p (b t) -> p b t", b=DEC_BATCH),
                                              out[rows, i, :, 4 * half:4 * half + 4])
                ins.then_inc(m["s_pv_taken"], 1)
                t0 = 0 if l == 0 else 6
                dve.wait_ge(m["s_cut"], 1)
                TT(h_lo[:, t0:8, 0:TS], oo[:, t0:8, :], h_hi[:, t0:8, 0:TS].bitcast(F32), ALU.subtract) \
                    .then_inc(m["s_done"], 1)

            def prompt_attention(l):
                m = mx[l]
                items = swa_items(l)
                se, st = (s_exp, stat) if l == 0 else (s_exp1, stat1)
                N = len(items)
                sums = [0, 0]

                def top(n):
                    kind, b, g = items[n]
                    s4 = n % 4
                    dve.wait_ge(m["scored"], n + 1)
                    out = banks(2 * (n % 2), 2, 768)
                    if n >= 4:
                        dve.wait_ge(m["normed"], n - 3)
                    if kind == "swa":
                        if n >= RING:
                            dve.wait_ge(m["pturned"], n - RING + 1)
                        w, nd0 = (BLOCK, BLOCK) if b == 0 else (256, 0)
                        for j in range(3):
                            STT(out=se[:, n % RING, j * 256:j * 256 + w], in0=nd_p[:, nd0:nd0 + w],
                                scalar=float(slopes[3 * g + j]), in1=out[:, j * 256:j * 256 + w],
                                op0=ALU.mult, op1=ALU.add).then_inc(m["biased"], 1)
                        sums[0] += 3
                        dve.wait_ge(m["biased"], sums[0])
                        src = se[:, n % RING, :].rearrange("p (j k) -> p j k", j=3)[:, :, 0:w]
                        dve.tensor_reduce(st[:, s4, 0, :], src, AX, ALU.max, negate=True).then_inc(m["maxed"], 1)
                        sums[1] += 1
                        dve.wait_ge(m["maxed"], sums[1])
                        TT(st[:, s4, 1, :], st[:, s4, 0, :], nsink_p[:, 3 * g:3 * g + 3], ALU.min) \
                            .then_inc(m["maxed2"], 1)
                        dve.wait_ge(m["maxed2"], sums[1])
                        TT(st[:, s4, 3, :], st[:, s4, 1, :], nsink_p[:, 3 * g:3 * g + 3], ALU.subtract) \
                            .then_inc(m["ready"], 1)
                    else:
                        src = ps[:, 2 * (n % 2):2 * (n % 2) + 2, 0:256]
                        dve.tensor_reduce(st[:, s4, 1, 0:2], src, AX, ALU.max, negate=True).then_inc(m["ready"], 1)

                swas = [0]

                def scale(n):
                    kind, b, g = items[n]
                    s4 = n % 4
                    dve.wait_ge(m["exped"], n + 1)
                    if kind == "swa":
                        TT(st[:, s4, 0, :], st[:, s4, 2, :], st[:, s4, 4, :], ALU.add).then_inc(m["summed"], 1)
                        swas[0] += 1
                        dve.wait_ge(m["summed"], swas[0])
                        dve.reciprocal(st[:, s4, 5, :], st[:, s4, 0, :]).then_inc(m["recip"], 1)
                    else:
                        dve.reciprocal(st[:, s4, 5, 0:2], st[:, s4, 2, 0:2]).then_inc(m["recip"], 1)

                def low(n):
                    dve.wait_ge(m["o_cut"], n + 1)
                    dst, src = o_view(items[n], n, h_lo)
                    hi, _ = o_view(items[n], n, h_hi)
                    TT(dst, src, hi.bitcast(F32), ALU.subtract).then_inc(m["o_done"], 1)

                for n in range(N + LAG + 2):
                    if 0 <= n - LAG - 2 < N:
                        low(n - LAG - 2)
                    if n < N:
                        top(n)
                    if 0 <= n - 1 < N:
                        scale(n - 1)
                    if l == 1 and 1 <= n < NB + 2:
                        w, t0 = (TS, 0) if n == 1 else (BLOCK, TS + (n - 2) * BLOCK)
                        dve.wait_ge(m["gate_cut"], n)
                        TT(h_lo[:, 0:6, t0:t0 + w], z[:, 0:6, t0:t0 + w], h_hi[:, 0:6, t0:t0 + w].bitcast(F32),
                           ALU.subtract).then_inc(m["gate_done"], 1)

            def ffn(l):
                r0 = R_FFN[l]
                h = r0 // 2
                v = lambda ap: ap.rearrange("p (b t) -> p b t", b=DEC_BATCH)

                def pieces(f, r, s):
                    ab = a_buf[:, s]
                    cs, cp = c_buf[:, s, 0:TS], c_buf[:, s, TS:T]
                    cc = conv_c[:, l, bass.ds(f, 1), :].rearrange("p o c -> p (o c)")

                    def tap(j, where, s_, val):
                        def run():
                            dve.wait_ge(s_, val)
                            if where == "p":
                                ins = STT(out=cp, in0=ab[:, 48 + j:48 + j + SEQ], scalar=cc[:, j:j + 1], in1=cp,
                                          op0=ALU.mult, op1=ALU.add)
                            else:
                                ins = STT(out=v(cs), in0=v(ab[:, 0:48])[:, :, j:j + DEC_SEQ], scalar=cc[:, j:j + 1],
                                          in1=v(cs), op0=ALU.mult, op1=ALU.add)
                            if j == 1:
                                ins.then_inc(conv1[l], 1)
                            elif where == "s":
                                ins.then_inc(conv_done[l], 1)
                        return run

                    def state():
                        dve.wait_ge(c0_done[l], f + 1)
                        dve.wait_ge(state_landed, 16 * (l + 1))
                        dve.tensor_copy(v(ab[:, 0:48])[:, :, 0:2],
                                        state_in[:, bass.ds(f, 1), :].rearrange("p o (b t) -> p (o b) t",
                                                                                b=DEC_BATCH)).then_inc(a_pre[l], 1)
                        so = state_out[:, bass.ds(f, 1), :]
                        dve.tensor_copy(so[:, :, 0:16].rearrange("p o (b t) -> p (o b) t", b=DEC_BATCH),
                                        v(ab[:, 0:48])[:, :, 4:6])
                        dve.tensor_copy(so[:, :, 16:18].rearrange("p o t -> p (o t)"),
                                        ab[:, 48 + SEQ:50 + SEQ]).then_inc(st_copied, 1)

                    def first():
                        state()
                        tap(1, "p", c0_done[l], f + 1)()

                    def second():
                        tap(1, "s", a_pre[l], f + 1)()

                    return [first, second, tap(0, "p", conv1[l], 2 * f + 2), tap(0, "s", conv1[l], 2 * f + 2)]

                def take(f, r, s, wide):
                    ab = a_buf[:, s]
                    for c in range(NCH):
                        dve.wait_ge(proj, 6 * r + c + 1)
                        if c == 0 and wide:
                            dve.wait_ge(conv_done[l], f - 1)
                        if c == 0:
                            dve.wait_ge(consts, 16 * NCONST)
                            TT(v(ab[:, 0:48])[:, :, 2:6], v(ps[:, 0, 0:TS]), v(rb[:, 0:TS]), ALU.mult)
                            ins = TT(ab[:, 50:50 + CH - TS], ps[:, 0, TS:CH], rb[:, TS:CH], ALU.mult)
                        else:
                            at = 50 + c * CH - TS
                            ins = TT(ab[:, at:at + CH], ps[:, c, 0:CH], rb[:, c * CH:(c + 1) * CH], ALU.mult)
                        ins.then_inc(freed[0], 1)

                def scale(f, s):
                    dve.wait_ge(silued[l], f + 1)
                    dve.wait_ge(consts, 16 * NCONST)
                    TT(c_buf[:, s], c_buf[:, s], rb[:, :], ALU.mult).then_inc(c_scaled[l], 1)

                def gated(f, r, s, c):
                    dve.wait_ge(proj, 6 * r + 3 + c + 1)
                    if c == 0:
                        dve.wait_ge(c_scaled[l], f + 1)
                    dve.wait_ge(consts, 16 * NCONST)
                    TT(g_f[:, c * CH:(c + 1) * CH], c_buf[:, s, c * CH:(c + 1) * CH], ps[:, 3 + c, 0:CH],
                       ALU.mult).then_inc(freed[1], 1)

                def low(f, s, c):
                    dve.wait_ge(g_cut[l], 3 * f + c + 1)
                    dve.wait_ge(consts, 16 * NCONST)
                    TT(g_lo[:, s, c * CH:(c + 1) * CH], g_f[:, c * CH:(c + 1) * CH],
                       g_hi[:, s, c * CH:(c + 1) * CH].bitcast(F32), ALU.subtract).then_inc(g_done[l], 1)

                def add(i, q):
                    oo, c = q // NCH, q % NCH
                    dve.wait_ge(dn_done, 24 * i + 24 * NG * l + q + 1)
                    xx = x[:, oo, c * CH:(c + 1) * CH]
                    TT(xx, xx, ps[:, 3 + (q + 1) % 5, 0:CH], ALU.add).then_inc(dn_added, 1)

                take(0, h, 0, False)
                for p in pieces(0, h, 0):
                    p()

                def group(i, last, first=False):
                    f, r = 2 * i, 2 * i + h
                    for s in range(2):
                        if s == 1:
                            take(f + 1, r + 1, 1, not first)
                            for p in pieces(f + 1, r + 1, 1):
                                p()
                        scale(f + s, s)
                        gated(f + s, r + s, s, 0)
                        gated(f + s, r + s, s, 1)
                        low(f + s, s, 0)
                        gated(f + s, r + s, s, 2)
                        low(f + s, s, 1)
                        low(f + s, s, 2)
                    if not last:
                        take(f + 2, r + 2, 0, True)
                    ps_ = [] if last else pieces(f + 2, r + 2, 0)
                    for q in range(KD * NCH):
                        add(i, q)
                        if last and l == 0 and q % NCH == 2:
                            low_of_h(2, q // NCH)
                        if q >= 5 and q % 3 == 2 and ps_:
                            ps_.pop(0)()

                group(0, False, first=True)
                with dve.Fori(1, NG - 1) as i:
                    group(i, False)
                group(NG - 1, True)
                if l == 0:
                    for e in range(KD, KD * NCH):
                        low_of_h(2, e)

            for l in range(2):
                m = mx[l]
                tiles = stat_tiles(l)
                nu, r0 = (IN_A, R_INA) if l == 0 else (IN_B, R_INB)
                norm_rstd(2 * l)
                for u in range(nu):
                    if l == 0 and u == Z_OVER_MEM:
                        dve.wait_ge(mem_vt, 2)
                        dve.wait_ge(mem_stored, 16)
                    for c in range(NCH):
                        dve.wait_ge(proj, 3 * (r0 + u) + c + 1)
                        if u == 0:
                            dve.wait_ge(rb_taken, NCH * 2 * l + c + 1)
                        cs = slice(c * CH, (c + 1) * CH)
                        TT(z[:, unit_tiles(l)[u], cs], ps[:, 3 * (u % 2) + c, 0:CH], rb[:, cs], ALU.mult) \
                            .then_inc(freed[u % 2], 1)
                        if l == 1 and u >= IN_B - 3:
                            q = NCH * (u - (IN_B - 3)) + c
                            _, _, bank, _, for_tiles = spread_b(q)
                            dve.wait_ge(m["z_spread"], q + 1)
                            for t in for_tiles:
                                zz = z[:, t, cs]
                                g_c = vgain[:, t - 6:t - 5] if t < 12 else qgain[:, 2:3]
                                STT(out=zz, in0=zz, scalar=g_c, in1=ps[:, bank, 0:CH], op0=ALU.mult,
                                    op1=ALU.mult).then_inc(m["z_normed"], 1)
                    if l == 1 and u == IN_B - 4:
                        dve.wait_ge(m["z_root"], 1)
                        dve.reciprocal(rstd[:, :], root[:, :]).then_inc(m["z_rstd"], 1)
                    if l == 0:
                        memory_step(u)
                if l == 0:
                    dve.wait_ge(m["z_root"], 1)
                    dve.reciprocal(rstd[:, :], root[:, :]).then_inc(m["z_rstd"], 1)
                    for q in range(30):
                        t, c = q // NCH, q % NCH
                        g_c = qgain[:, 0:1] if t < 6 else hgain[:, 1:2] if t < 8 else qgain[:, 1:2]
                        dve.wait_ge(m["z_spread"], q + 1)
                        zz = z[:, t, c * CH:(c + 1) * CH]
                        STT(out=zz, in0=zz, scalar=g_c, in1=ps[:, 1 + q % 5, 0:CH], op0=ALU.mult, op1=ALU.mult) \
                            .then_inc(m["z_normed"], 1)
                dve.wait_ge(m["z_normed"], 30 if l == 0 else 24)
                if l == 1:
                    dve.wait_ge(m["gate_in"], 16 * 4)
                    dve.wait_ge(m["gelud"], 12)
                    for q in range(NB + 1):
                        w, t0 = (TS, 0) if q == 0 else (BLOCK, TS + (q - 1) * BLOCK)
                        mv = mixed[:, q % 2, :].rearrange("p (t n) -> p t n", t=6)[:, :, 0:w]
                        dve.wait_ge(m["gate_mixed"], q + 1)
                        if q >= 2:
                            dve.wait_ge(m["gate_mult"], q - 1)
                        src = banks(2 + 2 * (q % 2), 2, 768).rearrange("p (t n) -> p t n", t=6)[:, :, 0:w]
                        TT(mv, src, (bb4 if q == 0 else bb)[:, :, :], ALU.add).then_inc(m["gate_biased"], 1)
                        dve.wait_ge(m["gate_biased"], q + 1)
                        zz = z[:, 0:6, t0:t0 + w]
                        TT(zz, mv, zz, ALU.mult).then_inc(m["gate_mult"], 1)
                sample_attention(l)
                prompt_attention(l)
                r0 = R_OUTA if l == 0 else R_OUTB
                def add_out(i, s, c):
                    dve.wait_ge(proj, 6 * i + 3 * (r0 + s) + c + 1)
                    xx = x[:, bass.ds(2 * i + s, 1), c * CH:(c + 1) * CH].rearrange("p o t -> p (o t)")
                    TT(xx, xx, ps[:, 3 * s + c, 0:CH], ALU.add).then_inc(freed[s], 1)

                with dve.Fori(0, OUT_U // 2 - 1) as i:
                    for s in range(2):
                        for c in range(NCH):
                            add_out(i, s, c)
                for c in range(NCH):
                    add_out(OUT_U // 2 - 1, 0, c)
                for c in range(NCH):
                    add_out(OUT_U // 2 - 1, 1, c)
                    for k in range(KD):
                        low_of_h(2 * l + 1, KD * c + k)
                norm_rstd(2 * l + 1)
                for s in range(2):
                    ins = dve.memset(a_buf[:, s, 48:50], 0.0)
                ins.then_inc(zeroed, 1)
                dve.wait_ge(zeroed, l + 1)
                dve.wait_ge(rb_taken, NCH * (2 * l + 2))
                ffn(l)


def kernel(**inputs):
    import math
    import numpy as np
    import concourse.bacc as _bacc
    from concourse import mybir as _mybir
    from concourse.bass_utils import run_bass_kernel_spmd as _run

    f4 = np.float32
    a = {k: np.asarray(v) for k, v in inputs.items()}

    def col_unit(w):
        return w.reshape(KD, P, P).transpose(1, 0, 2).reshape(P, KD * P)

    def col_units(w):
        return [col_unit(w[:, i * P:(i + 1) * P]) for i in range(w.shape[1] // P)]

    q_cols = np.concatenate([np.arange((6 * i + 3 * h + j) * HD, (6 * i + 3 * h + j + 1) * HD)
                             for i in range(2) for j in range(3) for h in range(2)])
    in_a_cols = np.concatenate([q_cols, np.arange(768, 1024), np.arange(1280, 1536), np.arange(1024, 1280)])
    out_a_rows = np.concatenate([q_cols, np.arange(768, 1024)])
    in_b_cols = np.concatenate([np.arange(t * P, (t + 1) * P) for t in unit_tiles(1)])
    stream = []
    for l in range(2):
        stream += col_units(a["w_mem_kv"][l])
    for l in range(2):
        stream += col_units(a["w_in_a"][0][:, in_a_cols] if l == 0 else a["w_in_b"][0][:, in_b_cols])
        stream += col_units(a["w_out_a"][0][out_a_rows] if l == 0 else a["w_out_b"][0])
        gate = col_units(a["w_ffn_in"][l][:, :D_FF])
        up = col_units(a["w_ffn_in"][l][:, D_FF:])
        down = list(a["w_down"][l].reshape(NF, P, D_MODEL))
        stream.append(gate[0])
        for g in range(NG):
            stream += [up[2 * g], gate[2 * g + 1], up[2 * g + 1]]
            if g < NG - 1:
                stream.append(gate[2 * g + 2])
            stream += [down[2 * g], down[2 * g + 1]]
    w = np.stack(stream)
    assert w.shape[0] == N_STREAM

    def feat(v, n):
        return v.T.reshape(n, P, -1).transpose(1, 0, 2)

    tokens = np.concatenate([a["x_sample"].reshape(TS, D_MODEL), a["x_prompt"].reshape(SEQ, D_MODEL)])
    tiles = lambda v: v.reshape(-1, P).T
    twice = lambda v: np.concatenate([v, v])
    gain = np.stack([tiles(a[n][l]) for n in ("norm1_g", "norm2_g", "mem_norm_g") for l in range(2)], 1)
    hgain = np.stack([twice(v) for v in (a["q_norm_a"][0], a["k_norm_a"][0], a["xq_norm"][0], a["xq_norm"][1],
                                         a["xk_norm"][0], a["xk_norm"][1])], 1)

    def pow2(m):
        return [(2.0 ** (-8.0 / m)) ** (i + 1) for i in range(m)]

    slopes = np.asarray(pow2(8) + pow2(16)[0::2][:4], f4)
    g_of, t_of, b_of = (np.arange(P) // 4) % 4, np.arange(P) % 4, np.arange(P) // 16
    cols = np.zeros((P, 8), f4)
    cols[:, 0] = EPS
    cols[:, 1] = 1.0 / HD
    cols[:, 2] = 1.0 / HD
    cols[ALL_ROW:96:32, 2] = 1.0 / 768
    for j in range(3):
        cols[:, 3 + j] = slopes[3 * g_of + j]
    sel = np.zeros((P, NSEL, 32), f4)
    for t in range(10):
        sel[:64, t, 2 * t] = 1
        sel[64:, t, 2 * t + 1] = 1
    sel[:, SEL_ALL, ALL_ROW] = 1
    sel_t = np.tile(sel.transpose(2, 1, 0), (3, 1, 1))
    NEG = -1e32
    dist = np.arange(P)[:, None] + BLOCK - np.arange(2 * BLOCK)[None]
    nd_p = np.where((dist >= 0) & (dist < BLOCK), -dist, NEG).astype(f4)
    key = np.arange(KEYS_S)[None]
    kb, kt = (key - BLOCK) // 4, (key - BLOCK) % 4
    dist = np.where(key < BLOCK, t_of[:, None] + BLOCK - key, t_of[:, None] - kt)
    ok = (dist >= 0) & (dist < BLOCK) & ((key < BLOCK) | (kb == b_of[:, None]))
    nd_s = np.where(ok, -dist, NEG).astype(f4)

    sinks = a["sinks_a"][0]
    ws = a["w_s_b"][0]
    ws4 = np.zeros((TS, 4, TS), f4)
    for b in range(DEC_BATCH):
        ws4[4 * b:4 * b + 4, :, 4 * b:4 * b + 4] = ws[:, :4, :4].transpose(2, 0, 1)
    bs = a["b_s_b"][0]
    grp = (2 * np.arange(6)[None] + np.arange(P)[:, None] // 64) // 3
    pairs = lambda v: v.reshape(v.shape[:-2] + (2, P))
    arrays = {
        "w": w,
        "x_t": feat(tokens, KD),
        "mem_t": feat(a["mem_prompt"].reshape(N_MEM, D_MODEL), KD),
        "ident": np.eye(P, dtype=f4), "sel": sel, "sel_t": sel_t, "gain": gain, "hgain": hgain,
        "vgain": tiles(a["v_norm_b"][0]), "cols": cols,
        "sink_p": np.broadcast_to(sinks, (P, 12)),
        "sink_s": np.stack([sinks[3 * g_of + j] for j in range(3)], 1),
        "conv_c": np.stack([np.stack([tiles(v) for v in (*a["conv_w"][l], a["conv_b"][l])], -1) for l in range(2)], 1),
        "nd_p": nd_p, "nd_s": nd_s,
        "s_k": pairs(a["cache_win_k"][0]).transpose(3, 2, 0, 1),
        "s_v": a["cache_win_v"][0].reshape(DEC_BATCH, BLOCK, 256).transpose(1, 0, 2),
        "s_mk": pairs(a["cache_mem_k"]).transpose(0, 4, 3, 1, 2),
        "s_mv": a["cache_mem_v"].reshape(2, DEC_BATCH, 2, P, 256).transpose(0, 3, 2, 1, 4),
        "ws_t": ws.transpose(2, 0, 1), "ws4": ws4,
        "bb": bs[grp], "bb4": np.tile(bs[grp][:, :, :4], (1, 1, DEC_BATCH)),
        "state": a["state_conv"].reshape(2, DEC_BATCH * 2, NF, P).transpose(0, 3, 2, 1),
        "cache_k": a["cache_win_k"][0].reshape(DEC_BATCH, BLOCK, 256),
        "cache_v": a["cache_win_v"][0].reshape(DEC_BATCH, BLOCK, 256),
    }
    arrays = {k: np.ascontiguousarray(v) for k, v in arrays.items()}
    nc = _bacc.Bacc("TRN2", target_bir_lowering=False, num_devices=1, dynamic_dma_scratch_size=1024)
    fp = _mybir.dt.float32
    d = {k: nc.dram_tensor(f"in_{k}", v.shape, fp, kind="ExternalInput").ap() for k, v in arrays.items()}
    out_shapes = {
        "y": (P, KD, T), "win_k_s": (DEC_BATCH, BLOCK, 256), "win_v_s": (DEC_BATCH, BLOCK, 256),
        "win_k_p": (P, 2, BLOCK), "win_v_p": (P, 2, BLOCK), "chunk_p": (P, 6, BLOCK), "chunk_s": (P, 6, TS),
        "mem_k": (P, 4, N_MEM), "mem_v": (P, 4, N_MEM), "state": (2, P, NF, 18),
    }
    o = {k: nc.dram_tensor(f"out_{k}", s, fp, kind="ExternalOutput").ap() for k, s in out_shapes.items()}
    hybrid_step(nc, d, o, slopes)
    r = _run(nc, [{f"in_{k}": v for k, v in arrays.items()}], core_ids=[0])
    g = {k: r.results[0][f"out_{k}"] for k in out_shapes}

    def rows(v):
        return v.transpose(2, 1, 0).reshape(v.shape[2], -1)

    y = rows(g["y"])
    win = lambda v: v.reshape(1, -1, BLOCK, A_KV, HD)
    mem = lambda v: np.stack([rows(v[:, 2 * l:2 * l + 2]) for l in range(2)]).reshape(2, 1, N_MEM, 4, HD)
    state = g["state"].transpose(0, 3, 2, 1).reshape(2, 18, D_FF)
    outs = (
        y[TS:].reshape(1, SEQ, D_MODEL), y[:TS].reshape(DEC_BATCH, DEC_SEQ, D_MODEL),
        win(rows(g["win_k_p"])), win(rows(g["win_v_p"])),
        rows(g["chunk_p"]).reshape(1, 1, BLOCK, 768),
        mem(g["mem_k"]), mem(g["mem_v"]),
        state[:, 16:].reshape(2, 1, 2, D_FF),
        win(g["win_k_s"]), win(g["win_v_s"]),
        rows(g["chunk_s"]).reshape(1, DEC_BATCH, DEC_SEQ, 768),
        state[:, :16].reshape(2, DEC_BATCH, 2, D_FF),
    )
    return tuple(np.ascontiguousarray(v) for v in outs)
```
